# Optimizing a Trainium2 kernel written in Bass

```python
import math
import jax
import jax.numpy as jnp
from jax import lax
import numpy as np

D_MODEL = 1024
BATCH = 1
SEQ = 128
DEPTH = 2
DEC_BATCH = 1
DEC_SEQ = 128
PAST_LEN = 128

GRID_W = 64
HD = 64
A_HEADS = 8
A_KV_HEADS = 2
A_GROUP = A_HEADS // A_KV_HEADS
WINDOW = 128
BLK = 128
B_HEADS = 4
B_HD = 64
C_HEADS = 8
C_NOPE = 64
C_ROPE = 32
C_V = 64
Q_LORA = 256
KV_LORA = 128
BRANCH_A = A_HEADS * HD
BRANCH_B = B_HEADS * 2 * B_HD
BRANCH_C = C_HEADS * C_V
IN_SPLITS = (A_HEADS * HD, A_KV_HEADS * HD, A_KV_HEADS * HD,
             B_HEADS * 2 * B_HD, B_HEADS * 2 * B_HD, B_HEADS * 2 * B_HD,
             Q_LORA, KV_LORA, C_ROPE, 3 * D_MODEL)
IN_COLS = sum(IN_SPLITS)
N_EXPERTS = 64
TOP_K = 6
N_GROUPS = 8
TOPK_GROUPS = 4
F_EXPERT = 256
F_SHARED = 256
ROUTED_SCALE = 2.5
QBLK = 128
ROPE_BASE = 10000.0
EPS = 1e-6
NEG = -1e30

kernel_name = "hybrid_diffusion_prefix_trunk_step"

def rms_norm(x, g):
    xf = x.astype(jnp.float32)
    y = xf * lax.rsqrt(jnp.mean(xf * xf, axis=-1, keepdims=True) + EPS)
    return (y * g.astype(jnp.float32)).astype(x.dtype)

def split_cols(z, sizes):
    offs, acc = [], 0
    for s in sizes[:-1]:
        acc += s
        offs.append(acc)
    return jnp.split(z, offs, axis=-1)

def rope_1d(x, pos):
    half = x.shape[-1] // 2
    inv = ROPE_BASE ** (-jnp.arange(half, dtype=jnp.float32) / half)
    ang = pos.astype(jnp.float32)[:, None] * inv[None, :]
    shape = (1, x.shape[1]) + (1,) * (x.ndim - 3) + (half,)
    cos = jnp.cos(ang).reshape(shape)
    sin = jnp.sin(ang).reshape(shape)
    xf = x.astype(jnp.float32)
    x1, x2 = xf[..., :half], xf[..., half:]
    return jnp.concatenate([x1 * cos - x2 * sin, x1 * sin + x2 * cos], axis=-1).astype(x.dtype)

def rope_2d(x):
    t = jnp.arange(x.shape[1])
    d = x.shape[-1] // 2
    return jnp.concatenate([rope_1d(x[..., :d], t // GRID_W), rope_1d(x[..., d:], t % GRID_W)], axis=-1)

def softmax_sink(s, sink):
    if sink is None:
        return jax.nn.softmax(s, axis=-1)
    m = jnp.maximum(jnp.max(s, axis=-1, keepdims=True), sink)
    e = jnp.exp(s - m)
    return e / (jnp.sum(e, axis=-1, keepdims=True) + jnp.exp(sink - m))

def dense_attn(q, k, v, sink=None):
    B, T, Hk, G, d = q.shape
    nb = T // QBLK
    scale = 1.0 / math.sqrt(d)
    qb = jnp.moveaxis(q.reshape(B, nb, QBLK, Hk, G, d), 1, 0)
    sk = None if sink is None else sink.astype(jnp.float32).reshape(1, Hk, G, 1, 1)

    def one(qi):
        s = jnp.einsum("bqhgd,bshd->bhgqs", qi, k).astype(jnp.float32) * scale
        p = softmax_sink(s, sk)
        return jnp.einsum("bhgqs,bshe->bqhge", p.astype(v.dtype), v)

    o = lax.map(one, qb)
    return jnp.moveaxis(o, 0, 1).reshape(B, T, Hk, G, v.shape[-1])

def window_attn(q, k, v, kc, vc, sink):
    B, T, Hk, G, d = q.shape
    nb = T // BLK
    scale = 1.0 / math.sqrt(d)
    pad = ((0, 0), (BLK, BLK), (0, 0), (0, 0))
    kp, vp = jnp.pad(k, pad), jnp.pad(v, pad)

    def bands(xp):
        return jnp.concatenate([xp[:, o:o + T].reshape(B, nb, BLK, Hk, xp.shape[-1]) for o in (0, BLK, 2 * BLK)], axis=2)

    kb, vb = bands(kp), bands(vp)
    qb = q.reshape(B, nb, BLK, Hk, G, d)
    s_loc = jnp.einsum("bnqhgd,bnkhd->bnhgqk", qb, kb).astype(jnp.float32) * scale
    qi = jnp.arange(BLK)[:, None]
    ki = jnp.arange(3 * BLK)[None, :] - BLK
    key_abs = jnp.arange(nb)[:, None, None] * BLK + ki[None]
    valid = (jnp.abs(qi - ki) <= WINDOW)[None] & (key_abs >= 0) & (key_abs < T)
    s_loc = jnp.where(valid[None, :, None, None], s_loc, NEG)
    s_ctx = jnp.einsum("bnqhgd,bshd->bnhgqs", qb, kc).astype(jnp.float32) * scale
    S = kc.shape[1]
    p = softmax_sink(jnp.concatenate([s_ctx, s_loc], axis=-1),
                     sink.astype(jnp.float32).reshape(1, 1, Hk, G, 1, 1)).astype(v.dtype)
    o = (jnp.einsum("bnhgqs,bshd->bnqhgd", p[..., :S], vc)
         + jnp.einsum("bnhgqk,bnkhd->bnqhgd", p[..., S:], vb))
    return o.reshape(B, T, Hk, G, d)

def mla_kv(ckv, kpe, w_ukv):
    B, S, _ = ckv.shape
    kv = (ckv @ w_ukv).reshape(B, S, C_HEADS, C_NOPE + C_V)
    k_nope, v = kv[..., :C_NOPE], kv[..., C_NOPE:]
    k = jnp.concatenate([k_nope, jnp.broadcast_to(kpe[:, :, None, :], (B, S, C_HEADS, C_ROPE))], axis=-1)
    return k, v

def token_mix(h, P, l, ctx=None):
    B, T, _ = h.shape
    z = h @ P["w_in"][l]
    qa, ka, va, qd, kd, vd, qc, kvc, kpe, gl = split_cols(z, IN_SPLITS)
    qa = qa.reshape(B, T, A_KV_HEADS, A_GROUP, HD)
    ka = ka.reshape(B, T, A_KV_HEADS, HD)
    va = va.reshape(B, T, A_KV_HEADS, HD)
    qd = qd.reshape(B, T, B_HEADS, 2, B_HD)
    kd = kd.reshape(B, T, B_HEADS, 2, B_HD)
    vd = vd.reshape(B, T, B_HEADS, 2 * B_HD)
    qm = (rms_norm(qc, P["mla_q_norm"][l]) @ P["mla_w_uq"][l]).reshape(B, T, C_HEADS, C_NOPE + C_ROPE)
    ckv = rms_norm(kvc, P["mla_kv_norm"][l])
    new_ctx = (ka, va, kd, vd, ckv, kpe)
    sink = P["swa_sink"][l].reshape(A_KV_HEADS, A_GROUP)
    w_ukv = P["mla_w_ukv"][l]
    if ctx is None:
        oa = dense_attn(qa, ka, va, sink)
        kd_all, vd_all = kd, vd
        km, vm = mla_kv(ckv, kpe, w_ukv)
    else:
        ka_c, va_c, kd_c, vd_c, ckv_c, kpe_c = ctx
        oa = window_attn(rope_2d(qa), rope_2d(ka), va, ka_c, va_c, sink)
        qd = rope_2d(qd)
        kd_all = jnp.concatenate([kd_c, rope_2d(kd)], axis=1)
        vd_all = jnp.concatenate([vd_c, vd], axis=1)
        qm = jnp.concatenate([qm[..., :C_NOPE], rope_2d(qm[..., C_NOPE:])], axis=-1)
        km_c, vm_c = mla_kv(ckv_c, kpe_c, w_ukv)
        km_l, vm_l = mla_kv(ckv, rope_2d(kpe), w_ukv)
        km = jnp.concatenate([km_c, km_l], axis=1)
        vm = jnp.concatenate([vm_c, vm_l], axis=1)
    lam_init = 0.8 - 0.6 * math.exp(-0.3 * l)
    lam = (jnp.exp(jnp.sum(P["dif_lq1"][l].astype(jnp.float32) * P["dif_lk1"][l].astype(jnp.float32)))
           - jnp.exp(jnp.sum(P["dif_lq2"][l].astype(jnp.float32) * P["dif_lk2"][l].astype(jnp.float32)))
           + lam_init)
    o1 = dense_attn(qd[:, :, :, 0:1], kd_all[:, :, :, 0], vd_all)
    o2 = dense_attn(qd[:, :, :, 1:2], kd_all[:, :, :, 1], vd_all)
    od = o1 - lam.astype(o1.dtype) * o2
    od = rms_norm(od[:, :, :, 0], P["dif_subln"][l]) * (1.0 - lam_init)
    om = dense_attn(qm[:, :, :, None], km, vm)
    ga, gb, gc = jnp.split(jax.nn.sigmoid(gl), 3, axis=-1)
    merged = (ga * (oa.reshape(B, T, BRANCH_A) @ P["w_branch_a"][l])
              + gb * (od.reshape(B, T, BRANCH_B) @ P["w_branch_b"][l])
              + gc * (om.reshape(B, T, BRANCH_C) @ P["w_branch_c"][l]))
    return merged @ P["w_out"][l], new_ctx

def moe(h, P, l):
    B, T, D = h.shape
    N = B * T
    x = h.reshape(N, D)
    scores = jax.nn.sigmoid((x @ P["router_w"][l]).astype(jnp.float32))
    biased = scores + P["router_bias"][l].astype(jnp.float32)
    grp = biased.reshape(N, N_GROUPS, N_EXPERTS // N_GROUPS)
    grp_score = jnp.sum(lax.top_k(grp, 2)[0], axis=-1)
    _, gidx = lax.top_k(grp_score, TOPK_GROUPS)
    gmask = jnp.sum(jax.nn.one_hot(gidx, N_GROUPS, dtype=jnp.float32), axis=1)
    emask = jnp.repeat(gmask, N_EXPERTS // N_GROUPS, axis=1) > 0
    _, eidx = lax.top_k(jnp.where(emask, biased, NEG), TOP_K)
    w = jnp.take_along_axis(scores, eidx, axis=-1)
    w = w / jnp.sum(w, axis=-1, keepdims=True) * ROUTED_SCALE
    gates = jnp.einsum("nk,nke->ne", w, jax.nn.one_hot(eidx, N_EXPERTS, dtype=jnp.float32)).astype(x.dtype)
    hid = (jax.nn.silu(jnp.einsum("nd,edf->nef", x, P["moe_w_gate"][l]))
           * jnp.einsum("nd,edf->nef", x, P["moe_w_up"][l]))
    routed = jnp.einsum("nef,efd->nd", hid * gates[:, :, None], P["moe_w_down"][l])
    shared = (jax.nn.silu(x @ P["shared_w_gate"][l]) * (x @ P["shared_w_up"][l])) @ P["shared_w_down"][l]
    return (routed + shared).reshape(B, T, D)

def layer(x, mod, P, l, ctx=None):
    sh1, sc1, g1, sh2, sc2, g2 = jnp.split(mod, 6, axis=-1)
    h = rms_norm(x, P["norm_attn_pre"][l]) * (1 + sc1) + sh1
    a, new_ctx = token_mix(h, P, l, ctx)
    x = x + g1 * rms_norm(a, P["norm_attn_post"][l])
    h = rms_norm(x, P["norm_ffn_pre"][l]) * (1 + sc2) + sh2
    x = x + g2 * rms_norm(moe(h, P, l), P["norm_ffn_post"][l])
    return x, new_ctx

def setup_inputs(seed: int = 0) -> dict:
    key = jax.random.key(seed)
    ks = iter(jax.random.split(key, 64))

    def nrm(shape, scale=1.0):
        return jax.random.normal(next(ks), shape, jnp.float32) * scale

    def gain(shape):
        return 1.0 + nrm(shape, 0.05)

    D = D_MODEL
    return {
        "x_prompt": nrm((BATCH, SEQ, D)),
        "x_sample": nrm((DEC_BATCH, DEC_SEQ, D)),
        "cache_swa_k": nrm((DEC_BATCH, DEPTH, PAST_LEN, A_KV_HEADS, HD)),
        "cache_swa_v": nrm((DEC_BATCH, DEPTH, PAST_LEN, A_KV_HEADS, HD)),
        "cache_dif_k": nrm((DEC_BATCH, DEPTH, PAST_LEN, B_HEADS, 2, B_HD)),
        "cache_dif_v": nrm((DEC_BATCH, DEPTH, PAST_LEN, B_HEADS, 2 * B_HD)),
        "cache_mla_ckv": nrm((DEC_BATCH, DEPTH, PAST_LEN, KV_LORA)),
        "cache_mla_kpe": nrm((DEC_BATCH, DEPTH, PAST_LEN, C_ROPE)),
        "c": nrm((DEC_BATCH, D)),
        "c_ctx": nrm((D,)),
        "w_mod": nrm((DEPTH, D, 6 * D), 0.5 * D ** -0.5),
        "b_mod": nrm((DEPTH, 6 * D), 0.02),
        "norm_attn_pre": gain((DEPTH, D)),
        "norm_attn_post": gain((DEPTH, D)),
        "norm_ffn_pre": gain((DEPTH, D)),
        "norm_ffn_post": gain((DEPTH, D)),
        "w_in": nrm((DEPTH, D, IN_COLS), D ** -0.5),
        "swa_sink": nrm((DEPTH, A_HEADS), 0.5),
        "dif_lq1": nrm((DEPTH, B_HD), 0.1),
        "dif_lk1": nrm((DEPTH, B_HD), 0.1),
        "dif_lq2": nrm((DEPTH, B_HD), 0.1),
        "dif_lk2": nrm((DEPTH, B_HD), 0.1),
        "dif_subln": gain((DEPTH, 2 * B_HD)),
        "mla_q_norm": gain((DEPTH, Q_LORA)),
        "mla_w_uq": nrm((DEPTH, Q_LORA, C_HEADS * (C_NOPE + C_ROPE)), Q_LORA ** -0.5),
        "mla_kv_norm": gain((DEPTH, KV_LORA)),
        "mla_w_ukv": nrm((DEPTH, KV_LORA, C_HEADS * (C_NOPE + C_V)), KV_LORA ** -0.5),
        "w_branch_a": nrm((DEPTH, BRANCH_A, D), BRANCH_A ** -0.5),
        "w_branch_b": nrm((DEPTH, BRANCH_B, D), BRANCH_B ** -0.5),
        "w_branch_c": nrm((DEPTH, BRANCH_C, D), BRANCH_C ** -0.5),
        "w_out": nrm((DEPTH, D, D), D ** -0.5),
        "router_w": nrm((DEPTH, D, N_EXPERTS), D ** -0.5),
        "router_bias": nrm((DEPTH, N_EXPERTS), 0.01),
        "moe_w_gate": nrm((DEPTH, N_EXPERTS, D, F_EXPERT), D ** -0.5),
        "moe_w_up": nrm((DEPTH, N_EXPERTS, D, F_EXPERT), D ** -0.5),
        "moe_w_down": nrm((DEPTH, N_EXPERTS, F_EXPERT, D), F_EXPERT ** -0.5),
        "shared_w_gate": nrm((DEPTH, D, F_SHARED), D ** -0.5),
        "shared_w_up": nrm((DEPTH, D, F_SHARED), D ** -0.5),
        "shared_w_down": nrm((DEPTH, F_SHARED, D), F_SHARED ** -0.5),
    }

def reference(x_prompt, x_sample, cache_swa_k, cache_swa_v, cache_dif_k, cache_dif_v,
              cache_mla_ckv, cache_mla_kpe, c, c_ctx, w_mod, b_mod,
              norm_attn_pre, norm_attn_post, norm_ffn_pre, norm_ffn_post, w_in, swa_sink,
              dif_lq1, dif_lk1, dif_lq2, dif_lk2, dif_subln, mla_q_norm, mla_w_uq,
              mla_kv_norm, mla_w_ukv, w_branch_a, w_branch_b, w_branch_c, w_out,
              router_w, router_bias, moe_w_gate, moe_w_up, moe_w_down,
              shared_w_gate, shared_w_up, shared_w_down):
    P = dict(norm_attn_pre=norm_attn_pre, norm_attn_post=norm_attn_post,
             norm_ffn_pre=norm_ffn_pre, norm_ffn_post=norm_ffn_post, w_in=w_in, swa_sink=swa_sink,
             dif_lq1=dif_lq1, dif_lk1=dif_lk1, dif_lq2=dif_lq2, dif_lk2=dif_lk2, dif_subln=dif_subln,
             mla_q_norm=mla_q_norm, mla_w_uq=mla_w_uq, mla_kv_norm=mla_kv_norm, mla_w_ukv=mla_w_ukv,
             w_branch_a=w_branch_a, w_branch_b=w_branch_b, w_branch_c=w_branch_c, w_out=w_out,
             router_w=router_w, router_bias=router_bias, moe_w_gate=moe_w_gate, moe_w_up=moe_w_up,
             moe_w_down=moe_w_down, shared_w_gate=shared_w_gate, shared_w_up=shared_w_up,
             shared_w_down=shared_w_down)
    y_p, y_s = x_prompt, x_sample
    states = [[], [], [], [], [], []]
    for l in range(DEPTH):
        mod_ctx = (jax.nn.silu(c_ctx) @ w_mod[l] + b_mod[l])[None, None, :]
        mod_lat = (jax.nn.silu(c) @ w_mod[l] + b_mod[l])[:, None, :]
        y_p, ctx_p = layer(y_p, mod_ctx, P, l)
        for i in range(6):
            states[i].append(ctx_p[i])
        cached = (cache_swa_k[:, l], cache_swa_v[:, l], cache_dif_k[:, l], cache_dif_v[:, l],
                  cache_mla_ckv[:, l], cache_mla_kpe[:, l])
        y_s, _ = layer(y_s, mod_lat, P, l, cached)
    state_swa_k = jnp.stack(states[0], axis=1)
    state_swa_v = jnp.stack(states[1], axis=1)
    state_dif_k = jnp.stack(states[2], axis=1)
    state_dif_v = jnp.stack(states[3], axis=1)
    state_mla_ckv = jnp.stack(states[4], axis=1)
    state_mla_kpe = jnp.stack(states[5], axis=1)
    return (y_p, y_s, state_swa_k, state_swa_v, state_dif_k, state_dif_v, state_mla_ckv, state_mla_kpe)


_drawn_inputs = setup_inputs


def setup_inputs(seed=0):
    import zlib

    import numpy as np

    out = dict(_drawn_inputs(seed))
    spreads = {}
    factors = {'swa_sink': 8.0, 'dif_lk1': 4.402, 'mla_q_norm': 3.3}
    for name, (base, spread) in spreads.items():
        noise = np.random.default_rng([zlib.crc32(name.encode()), seed]).standard_normal(out[name].shape)
        drawn = base * np.exp(spread * noise) if base else spread * noise
        out[name] = jnp.asarray(drawn.astype(out[name].dtype))
    for name, factor in factors.items():
        out[name] = (out[name] * factor).astype(out[name].dtype)
    return out
```

```python
import math
from contextlib import ExitStack

import numpy as np

import concourse.bass as bass
from concourse import mybir
from concourse.bass import ds

F32 = mybir.dt.float32
I32 = mybir.dt.int32
ALU = mybir.AluOpType
ACT = mybir.ActivationFunctionType
X = mybir.AxisListType.X

P = 128
D = 1024
KC = D // P
T = 256
DEPTH = 2
GRID_W = 64
ROPE_BASE = 10000.0
EPS = 1e-6
A_HEADS, A_KV, HD = 8, 2, 64
B_HEADS = 4
C_HEADS, C_NOPE, C_ROPE, C_V = 8, 64, 32, 64
C_QK = C_NOPE + C_ROPE
Q_LORA, KV_LORA = 256, 128
N_EXPERTS, N_GROUPS, TOP_K, TOPK_GROUPS, F_EXPERT = 64, 8, 6, 4, 256
ROUTED_SCALE = 2.5
CAP = 64
SLOTS = T * TOP_K
SB = 512
NSB = SLOTS // SB
XSW = CAP + SLOTS + CAP

QA, KA, VA = 0, 512, 640
QD, KD, VD = 768, 1280, 1792
QC, KVC, KPE, GL = 2304, 2560, 2688, 2720

RING_SLOTS = 12
LOADS = 60
EXPERT_LOADS = 3 * N_EXPERTS
ROUNDS = LOADS // RING_SLOTS
PASS_ROUNDS = EXPERT_LOADS // RING_SLOTS
L_MOD, L_QA, L_KVA, L_QD, L_KD, L_VD, L_QC = 0, 24, 26, 27, 29, 31, 33
L_GL01, L_UQ, L_GL, L_BR, L_OUT, L_SH = 34, 36, 37, 47, 53, 57

Z_JOBS, Z_QC, Z_KVC, Z_GL = 23, 9, 10, 11
PREP_JOBS = 25
NORMS = 7
UNITS = 18
XR = 2 * KC

VECTOR_STEPS = 254
PASS_STEPS = 98
TAIL_STEPS = 12

ATT = [(br, t, g) for br in "ABC" for t, n in ((0, 2), (1, 4)) for g in range(n)]


def projections_out(job):
    return job + 1 + (job >= 2) + (job >= Z_KVC)


def rope_tables(dim, rows, first):
    half = dim // 4
    inv = (np.float32(ROPE_BASE) ** (-np.arange(half, dtype=np.float32) / np.float32(half))).astype(np.float32)
    tok = np.arange(P)
    pos = np.stack([tok // GRID_W, tok % GRID_W]).astype(np.float32)
    cos, sin, swap = np.ones((P, P), np.float32), np.zeros((P, P), np.float32), np.zeros((P, P), np.float32)
    for r in range(first, rows):
        j = (r - first) % dim
        axis, i = j // (2 * half), j % (2 * half)
        angle = pos[axis] * inv[i % half]
        cos[r], sin[r] = np.cos(angle), np.sin(angle)
        if i < half:
            swap[r + half, r] = -1.0
        else:
            swap[r - half, r] = 1.0
    return cos, sin, swap


CONSTS = ("ident", "ones", "before", "cos_ab", "sin_ab", "swap_ab", "cos_c", "sin_c", "swap_c")


def constants():
    tables = [np.eye(P, dtype=np.float32), np.ones((P, P), np.float32),
              np.triu(np.ones((P, P), np.float32), 1)]
    tables += rope_tables(HD, P, 0)
    tables += rope_tables(C_ROPE, C_QK, C_NOPE)
    tables.append(np.tile(np.arange(SB, dtype=np.float32), (P, 1)))
    lam = [[0.8 - 0.6 * math.exp(-0.3 * l), 1.0 - (0.8 - 0.6 * math.exp(-0.3 * l))] for l in range(DEPTH)]
    return np.concatenate(tables, axis=1), np.array(lam, np.float32)


def hybrid_layers(nc, a, o):
    with ExitStack() as ctx:
        def sb(name, shape, dt=F32):
            return ctx.enter_context(nc.sbuf_tensor(name, shape, dt))

        def sem(name):
            return ctx.enter_context(nc.semaphore(name))

        PS = ctx.enter_context(nc.psum_tensor("PS", [P, 8, 512], F32))

        ring = sb("ring", [P, RING_SLOTS, 2048])
        xT = sb("xT", [P, KC, T])
        const = sb("const", [P, len(CONSTS) * P + SB])
        cst = {n: const[:, i * P:(i + 1) * P] for i, n in enumerate(CONSTS)}
        iota = const[:, len(CONSTS) * P:len(CONSTS) * P + SB]
        ident, ones, before = cst["ident"], cst["ones"], cst["before"]
        condT = sb("condT", [P, KC, 2])
        parT = sb("parT", [P, 84])
        modT = sb("modT", [P, 48, 2])
        pre1 = sb("pre1", [P, KC, 2])
        post1 = sb("post1", [P, KC, 2])
        pre2 = sb("pre2", [P, KC, 2])
        post2 = sb("post2", [P, KC, 2])
        sink = sb("sink", [P, A_HEADS])
        nsink = sb("nsink", [P, A_HEADS])
        rbias = sb("rbias", [P, N_EXPERTS])
        lamc = sb("lamc", [P, 2])
        lame = sb("lame", [P, 4])
        subl = sb("subl", [P, 1])
        condE = sb("condE", [P, KC, 2])
        negm = sb("negm", [P, 2, 4])
        psums = sb("psums", [P, 2, 4])
        sinke = sb("sinke", [P, 2, 4])
        prec = sb("prec", [P, 2, 4])
        sel = sb("sel", [P, 2, N_EXPERTS])
        gatew = sb("gatew", [P, 2, N_EXPERTS])
        rank = sb("rank", [P, 2, N_EXPERTS])
        count = sb("count", [P, N_EXPERTS])
        npass_i = sb("npass_i", [P, 1], I32)
        off_i = sb("off_i", [P, N_EXPERTS], I32)

        region = sb("region", [P, 23584])

        def view(at, *dims):
            n = math.prod(dims)
            v = region[:, at:at + n]
            if len(dims) == 2:
                return v.rearrange("p (a b) -> p a b", a=dims[0])
            if len(dims) == 3:
                return v.rearrange("p (a b c) -> p a b c", a=dims[0], b=dims[1])
            return v

        gates = view(0, 24, T)
        sq_x = view(0, KC, T)
        w_kvk = view(2048, KC, KV_LORA + C_ROPE)
        st_kb = view(3328, 512)
        st_ka = view(3840, P)
        st_ckv = view(3968, P)
        st_kpe = view(4096, C_QK)
        w_ukv = view(4192, C_HEADS, C_NOPE + C_V)
        qcT = view(5216, 2, T)
        kvcT = view(5728, T)
        hT = view(6144, KC, T)
        qA = view(8192, 4, T)
        qB = view(9216, 4, T)
        qC = view(10240, C_HEADS, T)
        kA = view(12288, 384)
        kB = view(12672, B_HEADS, 384)
        kC = view(14208, C_HEADS, 384)
        vA = view(17280, 3, P)
        vB = view(17664, 3, 512)
        vC = view(19200, 3, 512)
        sq_lora = view(19200, 3, T)
        prob = view(20736, 2, 512)
        probT = view(21760, 2, 512)
        rope_t = view(20736, 512)
        lam_in = view(21248, 4, HD)
        lam_t = view(21504, 2, HD)
        qcn = view(21760, 2, T)
        ckvT = view(22272, 384)
        state = view(22784, 800)
        sq_od = view(20736, 4, T)
        merged = view(12288, KC, T)
        merge_t = view(22272, 2, T)
        rw = view(21760, KC, N_EXPERTS)
        aT = view(17280, KC, T)
        sq_a = view(6144, KC, T)
        xs = view(0, KC, XSW)
        htok = view(13312, 2, D)
        gsel = view(15360, 2, SB)
        gval = view(16384, 2, SB)
        h2T = view(17408, KC, T)
        gvalT = view(17408, SLOTS // P, T)
        otok = view(15360, 2, D)
        yT = view(20480, KC, T)
        hid = view(22528, 2, 2, CAP)
        sig = view(22784, 2, 2 * CAP)
        act_g = view(23040, 2 * CAP)
        ssig = view(15360, 2, T)
        r_score, r_bias = view(2048, 2, N_EXPERTS), view(2176, 2, N_EXPERTS)
        r_top = view(2304, 2 * N_GROUPS, 8)
        r_gs, r_grep = view(2432, 2, 12), view(2456, 2, 12)
        r_g8, r_gm = view(2480, 2, 8), view(2496, 2, 8)
        r_mask, r_mrep = view(2512, 2, 66), view(2644, 2, 66)
        r_m8, r_sum = view(2776, 2, 8), view(2792, 2)
        r_most, r_np = view(2794, 1), view(2795, 1)

        r_selp, r_val, r_gwp = view(12288, 2, N_EXPERTS), view(12416, 2, N_EXPERTS), view(12544, 2, N_EXPERTS)
        r_cnt, r_junk = view(12672, N_EXPERTS), view(12736, N_EXPERTS)
        r_tmp = view(22528, SB)
        r_scan, r_pos, r_wk = view(23168, 2, 96), view(23360, 2, 8), view(23376, 2, 8)

        def norm_scratch(at, n):
            return [region[:, at + i * n:at + (i + 1) * n] for i in range(3)]

        ring_in = [sem(f"ring_in{i}") for i in range(RING_SLOTS)]
        ring_free = sem("ring_free")
        start_in, consts_in = sem("start_in"), sem("consts_in")
        params_in, weights_in, caches_in, lam_loaded, rw_in = (
            sem("params_in"), sem("weights_in"), sem("caches_in"), sem("lam_loaded"), sem("rw_in"))
        x_ready = sem("x_ready")
        start_tr, cond_exp, cond_ready = sem("start_tr"), sem("cond_exp"), sem("cond_ready")
        mod_done, params_tr, mod_ready = sem("mod_done"), sem("params_tr"), sem("mod_ready")
        sq_ready, ssq_ready, ssq_read, lora_ready = (
            sem("sq_ready"), sem("ssq_ready"), sem("ssq_read"), sem("lora_ready"))
        hn_ready, h_ready = sem("hn_ready"), sem("h_ready")
        z_done, z_ev = sem("z_done"), sem("z_ev")
        gate_ready = sem("gate_ready")
        prep_done, prep_ev = sem("prep_done"), sem("prep_ev")
        sink_exp = sem("sink_exp")
        lam_dot, lam_exp = sem("lam_dot"), sem("lam_exp")
        scores_done, negm_ready, prob_exp, prob_ready, prob_tr, probT_ready, pv_done, o_ready = (
            sem("scores_done"), sem("negm_ready"), sem("prob_exp"), sem("prob_ready"), sem("prob_tr"),
            sem("probT_ready"), sem("pv_done"), sem("o_ready"))
        od_ready = sem("od_ready")
        branch_done, merged_ready = sem("branch_done"), sem("merged_ready")
        wout_done, a_ready, x1_ready = sem("wout_done"), sem("a_ready"), sem("x1_ready")
        router_done, route_exp = sem("router_done"), sem("route_exp")
        htok_tr, htok_ready = sem("htok_tr"), sem("htok_ready")
        shared_gu, shared_exp, shared_hid, shared_down, y_shared = (
            sem("shared_gu"), sem("shared_exp"), sem("shared_hid"), sem("shared_down"), sem("y_shared"))
        sel_ready, rank_done, npass_ready, off_ready = (
            sem("sel_ready"), sem("rank_done"), sem("npass_ready"), sem("off_ready"))
        g_ready, gvt_tr, gvt_ready, gather_done, xs_ready, pad_set = (
            sem("g_ready"), sem("gvt_tr"), sem("gvt_ready"), sem("gather_done"), sem("xs_ready"), sem("pad_set"))
        gu_done, sig_ready, hid_ready, down_done, out_ready = (
            sem("gu_done"), sem("sig_ready"), sem("hid_ready"), sem("down_done"), sem("out_ready"))
        otok_tr, otok_ready, comb_done, y_ready = (
            sem("otok_tr"), sem("otok_ready"), sem("comb_done"), sem("y_ready"))
        vector_step = sem("vector_step")
        pass_step, expert_step, tail_step, start_step = (
            sem("pass_step"), sem("expert_step"), sem("tail_step"), sem("start_step"))
        state_out, taken = sem("state_out"), sem("taken")
        end_tr, end_ev, y_out = sem("end_tr"), sem("end_ev"), sem("y_out")

        block = ctx.enter_context(nc.Block())

        w_in, w_mod = a["w_in"], a["w_mod"]

        def at_layer(ap, l):
            return ap[ds(l, 1)]

        def cols(ap, l, c0, n):
            return at_layer(ap, l)[:, :, c0:c0 + n].rearrange("o (k p) n -> p (o k) n", p=P)

        def slot_cols(n, width):
            return ring[:, n % RING_SLOTS, 0:KC * width].rearrange("p (k n) -> p k n", k=KC)

        def wide(n):
            return ring[:, n % RING_SLOTS, :].rearrange("p (k n) -> p k n", k=4)

        def down_slot(n):
            return ring[:, n % RING_SLOTS, :].rearrange("p (f n) -> p f n", f=2)

        def apart(engine):
            engine.sem_inc(taken, 1)

        @block.sync
        def _(sp):
            passes = sp.alloc_register("sp_passes")
            sp.reg_mov(passes, 0)
            with sp.Fori(0, DEPTH) as l:
                rounds = sp.snap(l * ROUNDS + sp.snap(passes, min_val=0, max_val=8) * PASS_ROUNDS)

                def load(n, dst, src, base=rounds):
                    sp.wait_ge(ring_free, (base + n // RING_SLOTS) * RING_SLOTS + n % RING_SLOTS + 1)
                    sp.dma_start(dst, src).then_inc(ring_in[n % RING_SLOTS], 16)

                for j in range(24):
                    load(L_MOD + j, slot_cols(L_MOD + j, 256), cols(w_mod, l, 256 * j, 256))
                for j in range(2):
                    w = slot_cols(L_QA + j, 256)
                    for m in range(4):
                        dst, src = w[:, :, m * HD:(m + 1) * HD], cols(w_in, l, QA + 256 * (m % 2) + HD * (2 * j + m // 2), HD)
                        if m == 0:
                            load(L_QA + j, dst, src)
                        else:
                            sp.dma_start(dst, src).then_inc(ring_in[(L_QA + j) % RING_SLOTS], 16)
                load(L_KVA, slot_cols(L_KVA, 256), cols(w_in, l, KA, 256))
                for first, c0 in ((L_QD, QD), (L_KD, KD), (L_VD, VD)):
                    for j in range(2):
                        load(first + j, slot_cols(first + j, 256), cols(w_in, l, c0 + 256 * j, 256))
                load(L_QC, slot_cols(L_QC, 256), cols(w_in, l, QC, 256))
                for j in range(2):
                    load(L_GL01 + j, slot_cols(L_GL01 + j, 256), cols(w_in, l, GL + 256 * j, 256))
                load(L_UQ, ring[:, L_UQ % RING_SLOTS, 0:2 * C_HEADS * C_QK].rearrange("p (k n) -> p k n", k=2),
                     at_layer(a["mla_w_uq"], l).rearrange("o (k p) n -> p (o k) n", p=P))
                for j in range(10):
                    load(L_GL + j, slot_cols(L_GL + j, 256), cols(w_in, l, GL + 256 * (j + 2), 256))
                for half in range(2):
                    for b, name in enumerate(("w_branch_a", "w_branch_b", "w_branch_c")):
                        n = L_BR + 3 * half + b
                        load(n, wide(n), at_layer(a[name], l)[:, :, 512 * half:512 * half + 512].rearrange("o (k p) n -> p (o k) n", p=P))
                for j in range(4):
                    load(L_OUT + j, slot_cols(L_OUT + j, 256), cols(a["w_out"], l, 256 * j, 256))
                load(L_SH, slot_cols(L_SH, 256), cols(a["shared_w_gate"], l, 0, 256))
                load(L_SH + 1, slot_cols(L_SH + 1, 256), cols(a["shared_w_up"], l, 0, 256))
                load(L_SH + 2, down_slot(L_SH + 2), at_layer(a["shared_w_down"], l).rearrange("o (f p) n -> p (o f) n", p=P))

                def in_proj(name, e):
                    return at_layer(a[name], l)[:, ds(e, 1)].rearrange("o e (k p) n -> p (o e k) n", p=P)

                def experts_pass(base):
                    def load_gate_up(n, e, base=base):
                        load(n, slot_cols(n, 256), in_proj("moe_w_gate", e), base)
                        load(n + 1, slot_cols(n + 1, 256), in_proj("moe_w_up", e), base)

                    def load_down(n, e, base=base):
                        load(n, down_slot(n), at_layer(a["moe_w_down"], l)[:, ds(e, 1)].rearrange("o e (f p) n -> p (o e f) n", p=P), base)

                    load_gate_up(0, 0)
                    with sp.Fori(0, N_EXPERTS // 4 - 1) as i:
                        for u in range(4):
                            load_gate_up(2 + 3 * u, i * 4 + (u + 1), base + i)
                            load_down(4 + 3 * u, i * 4 + u, base + i)
                    for u in range(4):
                        e = N_EXPERTS - 4 + u
                        if u < 3:
                            load_gate_up(2 + 3 * e, e + 1)
                        load_down(4 + 3 * e - 2 * (u == 3), e)

                experts_pass(rounds + ROUNDS)
                sp.wait_ge(npass_ready, l + 1)
                apart(sp)
                npass = sp.value_load(npass_i[0:1, 0:1], min_val=1, max_val=4)
                with sp.If(npass > 1):
                    with sp.Fori(1, npass) as p:
                        experts_pass(rounds + ROUNDS + p * PASS_ROUNDS)
                    sp.nop()
                sp.reg_add(passes, passes, npass)
                sp.nop()

        @block.gpsimd
        def _(pool):
            stage = view(0, 2, D)
            crow = view(2048, D)
            pool.dma_start(const[:], a["consts"]).then_inc(consts_in, 16)
            pool.dma_start(stage[:, 0, :], a["x_prompt"][0]).then_inc(start_in, 16)
            pool.dma_start(stage[:, 1, :], a["x_sample"][0]).then_inc(start_in, 16)
            pool.dma_start(crow[0:KC, 0:P], a["c_ctx"].rearrange("(k p) -> k p", p=P)).then_inc(start_in, 16)
            pool.dma_start(crow[KC:2 * KC, 0:P], a["c"].rearrange("o (k p) -> (o k) p", p=P)).then_inc(start_in, 16)
            pool.wait_ge(start_tr, 5)
            with pool.Fori(0, DEPTH) as l:
                pool.wait_ge(x_ready, (l + 1) * XR)
                apart(pool)
                prow = view(20736 + 896, P)
                r = 0
                for name, n in (("b_mod", 48), ("norm_attn_pre", 8), ("norm_attn_post", 8), ("norm_ffn_pre", 8),
                                ("norm_ffn_post", 8), ("mla_q_norm", 2), ("mla_kv_norm", 1), ("dif_subln", 1)):
                    pool.dma_start(prow[r:r + n, :], at_layer(a[name], l).rearrange("o (k p) -> (o k) p", p=P)).then_inc(params_in, 16)
                    r += n
                pool.dma_start(sink[:], at_layer(a["swa_sink"], l).broadcast_to([P, A_HEADS])).then_inc(params_in, 16)
                pool.dma_start(rbias[:], at_layer(a["router_bias"], l).broadcast_to([P, N_EXPERTS])).then_inc(params_in, 16)
                pool.dma_start(lamc[:], at_layer(a["lam_consts"], l).broadcast_to([P, 2])).then_inc(params_in, 16)
                for i, name in enumerate(("dif_lq1", "dif_lq2", "dif_lk1", "dif_lk2")):
                    pool.dma_start(lam_in[:, i, :], at_layer(a[name], l).broadcast_to([P, HD])).then_inc(lam_loaded, 16)
                pool.dma_start(st_kb, at_layer(a["cache_dif_k"][0], l).rearrange("o s h m d -> s (o h m d)")).then_inc(caches_in, 16)
                pool.dma_start(st_ka, at_layer(a["cache_swa_k"][0], l).rearrange("o s h d -> s (o h d)")).then_inc(caches_in, 16)
                pool.dma_start(st_ckv, at_layer(a["cache_mla_ckv"][0], l).rearrange("o s d -> s (o d)")).then_inc(caches_in, 16)
                pool.dma_start(st_kpe[:, 0:C_NOPE], at_layer(a["cache_mla_ckv"][0], l)[:, :, 0:C_NOPE].rearrange("o s d -> s (o d)")).then_inc(caches_in, 16)
                pool.dma_start(st_kpe[:, C_NOPE:C_QK], at_layer(a["cache_mla_kpe"][0], l).rearrange("o s d -> s (o d)")).then_inc(caches_in, 16)
                pool.dma_start(vA[:, 2, :], at_layer(a["cache_swa_v"][0], l).rearrange("o s h d -> s (o h d)")).then_inc(caches_in, 16)
                pool.dma_start(vB[:, 2, :], at_layer(a["cache_dif_v"][0], l).rearrange("o s h d -> s (o h d)")).then_inc(caches_in, 16)
                pool.dma_start(w_kvk, cols(w_in, l, KVC, KV_LORA + C_ROPE)).then_inc(weights_in, 16)
                pool.dma_start(w_ukv.rearrange("p h n -> p (h n)"), at_layer(a["mla_w_ukv"], l).rearrange("o p n -> p (o n)")).then_inc(weights_in, 16)
                pool.wait_ge(z_ev, l * projections_out(Z_JOBS - 1) + projections_out(8))
                apart(pool)
                pool.dma_start(at_layer(o["swa_v"][0], l).rearrange("o s h d -> s (o h d)"), vA[:, 0, :]).then_inc(state_out, 16)
                pool.dma_start(at_layer(o["dif_v"][0], l).rearrange("o s h d -> s (o h d)"), vB[:, 0, :]).then_inc(state_out, 16)
                pool.wait_ge(prep_ev, l * PREP_JOBS + 14)
                apart(pool)
                pool.dma_start(at_layer(o["dif_k"][0], l).rearrange("o s h m d -> s (o h m d)"), state[:, 0:512]).then_inc(state_out, 16)
                pool.dma_start(at_layer(o["swa_k"][0], l).rearrange("o s h d -> s (o h d)"), state[:, 512:640]).then_inc(state_out, 16)
                pool.dma_start(at_layer(o["ckv"][0], l).rearrange("o s d -> s (o d)"), state[:, 640:768]).then_inc(state_out, 16)
                pool.dma_start(at_layer(o["kpe"][0], l).rearrange("o s d -> s (o d)"), state[:, 768:800]).then_inc(state_out, 16)
                pool.wait_ge(pv_done, l * UNITS + UNITS)
                apart(pool)
                pool.dma_start(rw, cols(a["router_w"], l, 0, N_EXPERTS)).then_inc(rw_in, 16)
            pool.wait_ge(state_out, DEPTH * 6 * 16)
            fin = view(0, 2, D)
            pool.wait_ge(end_ev, 4)
            pool.dma_start(o["y_prompt"][0], fin[:, 0, :]).then_inc(y_out, 16)
            pool.dma_start(o["y_sample"][0], fin[:, 1, :]).then_inc(y_out, 16)
            pool.wait_ge(y_out, 32)

        @block.tensor
        def _(pe):
            stage = view(0, 2, D)
            crow = view(2048, D)

            def transpose(out, in_, n=P):
                return pe.transpose(out, in_, ident[0:n, 0:n])

            pe.wait_ge(consts_in, 16)
            pe.wait_ge(start_in, 64)
            for j in range(4):
                for c in range(2):
                    for t in range(2):
                        ch = 2 * j + c
                        last = transpose(PS[:, j, (2 * c + t) * P:(2 * c + t + 1) * P], stage[:, t, ch * P:(ch + 1) * P])
                last.then_inc(start_tr, 1)
            transpose(PS[:, 4, 0:2 * KC], crow[0:2 * KC, 0:P], 2 * KC).then_inc(start_tr, 1)
            pe.sem_inc(ring_free, RING_SLOTS)
            pe.wait_ge(cond_ready, 1)

            passes = pe.alloc_register("pe_passes")
            pe.reg_mov(passes, 0)
            with pe.Fori(0, DEPTH) as l:
                before_l = pe.snap(passes, min_val=0, max_val=8)
                rounds = pe.snap(l * ROUNDS + before_l * PASS_ROUNDS)

                def arrived(n, base=None):
                    count = (rounds if base is None else base) + (n // RING_SLOTS + 1)
                    if n % RING_SLOTS < 2:
                        count = count + l * 3 + 3 * (base is not None or n >= L_QA)
                    pe.wait_ge(ring_in[n % RING_SLOTS], count * 16)

                def sum_squares(n, src, chunks, out):
                    pe.wait_ge(sq_ready, l * NORMS + n + 1)
                    for c in range(chunks):
                        last = pe.matmul(out, ones, src[:, c, :], start=(c == 0), stop=(c == chunks - 1))
                    return last

                pe.wait_ge(x_ready, (l + 1) * XR)
                for j in range(24):
                    arrived(L_MOD + j)
                    w = slot_cols(L_MOD + j, 256)
                    for m in range(2):
                        for k in range(KC):
                            last = pe.matmul(PS[:, 7, 4 * j + 2 * m:4 * j + 2 * m + 2], w[:, k, m * P:(m + 1) * P], condT[:, k, :],
                                             start=(k == 0), stop=(k == KC - 1))
                    if j == 23:
                        last.then_inc(mod_done, 1)
                    else:
                        last.then_inc(ring_free, 1)
                    if j == 0:
                        sum_squares(0, sq_x, KC, PS[:, 0, 0:T]).then_inc(ssq_ready, 1)
                        pe.wait_ge(params_in, (l + 1) * 11 * 16)
                        prow = view(20736 + 896, P)
                        transpose(PS[:, 6, 0:84], prow[0:84, :], 84).then_inc(params_tr, 1)
                        pe.wait_ge(caches_in, (l + 1) * 7 * 16)
                        for h in range(4):
                            last = transpose(PS[:, 2, h * P:(h + 1) * P], st_kb[:, h * P:(h + 1) * P])
                        last.then_inc(prep_done, 1)
                        transpose(PS[:, 3, 0:P], st_ka)
                        transpose(PS[:, 3, P:2 * P], st_ckv)
                        transpose(PS[0:C_QK, 3, 2 * P:3 * P], st_kpe).then_inc(prep_done, 1)

                def release(first, loads=1):
                    first.then_inc(ring_free, loads)

                def bank_emptied(j):
                    if j >= 2:
                        pe.wait_ge(z_ev, l * projections_out(Z_JOBS - 1) + projections_out(j - 2))

                def project(j, n, releases=1):
                    arrived(n)
                    bank_emptied(j)
                    w = slot_cols(n, 256)
                    for m in range(2):
                        for k in range(KC):
                            last = pe.matmul(PS[:, j % 2, m * T:(m + 1) * T], w[:, k, m * P:(m + 1) * P], hT[:, k, :],
                                             start=(k == 0), stop=(k == KC - 1))
                            if m == 0 and k == 0 and releases:
                                release(last)
                    last.then_inc(z_done, 1)

                for j in range(2):
                    arrived(L_QA + j)
                    bank_emptied(j)
                    w = slot_cols(L_QA + j, 256)
                    for m in range(2):
                        for k in range(KC):
                            if j == 0 and m == 0:
                                pe.wait_ge(h_ready, (l * 2 * KC + k + 1) * 2)
                            last = pe.matmul(PS[:, j, m * T:(m + 1) * T], w[:, k, m * P:(m + 1) * P], hT[:, k, :],
                                             start=(k == 0), stop=(k == KC - 1))
                            if m == 0 and k == 0:
                                release(last)
                    last.then_inc(z_done, 1)
                arrived(L_KVA)
                bank_emptied(2)
                w = slot_cols(L_KVA, 256)
                for k in range(KC):
                    last = pe.matmul(PS[:, 0, 0:T], w[:, k, 0:P], hT[:, k, :], start=(k == 0), stop=(k == KC - 1))
                    if k == 0:
                        release(last)
                for t in range(2):
                    for k in range(KC):
                        last = pe.matmul(PS[:, 0, T + t * P:T + (t + 1) * P], hT[:, k, t * P:(t + 1) * P], w[:, k, P:2 * P],
                                         start=(k == 0), stop=(k == KC - 1))
                last.then_inc(z_done, 1)
                for j in range(3, 7):
                    project(j, L_QD + j - 3)
                for j in (7, 8):
                    arrived(L_VD + j - 7)
                    bank_emptied(j)
                    w = slot_cols(L_VD + j - 7, 256)
                    for t in range(2):
                        for k in range(KC):
                            last = pe.matmul(PS[:, j % 2, t * T:(t + 1) * T], hT[:, k, t * P:(t + 1) * P], w[:, k, :],
                                             start=(k == 0), stop=(k == KC - 1))
                            if t == 0 and k == 0:
                                release(last)
                    last.then_inc(z_done, 1)
                project(Z_QC, L_QC)
                pe.wait_ge(weights_in, (l + 1) * 2 * 16)
                bank_emptied(Z_KVC)
                for k in range(KC):
                    last = pe.matmul(PS[:, 0, 0:T], w_kvk[:, k, 0:P], hT[:, k, :], start=(k == 0), stop=(k == KC - 1))
                    if k == 0:
                        release(last)
                for k in range(KC):
                    last = pe.matmul(PS[0:C_QK, 0, T:2 * T], w_kvk[:, k, C_NOPE:C_NOPE + C_QK], hT[:, k, :],
                                     start=(k == 0), stop=(k == KC - 1))
                last.then_inc(z_done, 1)

                def gate_job(g):
                    project(Z_GL + g, L_GL01 + g if g < 2 else L_GL + g - 2, g > 0)

                def projected(j):
                    pe.wait_ge(z_ev, l * projections_out(Z_JOBS - 1) + projections_out(j))

                def prep_bank(i):
                    if i >= 5:
                        pe.wait_ge(prep_ev, l * PREP_JOBS + i - 4)
                    return 2 + i % 5

                gate_job(0)
                projected(6)
                for i, src in ((2, qA[:, :, P:T]), (3, qB[:, :, P:T]), (4, kB[:, :, P:T])):
                    b = prep_bank(i)
                    pe.matmul(PS[:, b, :], cst["swap_ab"], src, start=True, stop=True).then_inc(prep_done, 1)
                projected(Z_KVC)
                b = prep_bank(5)
                pe.matmul(PS[:, b, 0:P], cst["swap_ab"], kA[:, P:T], start=True, stop=True)
                pe.matmul(PS[0:C_QK, b, P:T], cst["swap_c"][0:C_QK, 0:C_QK], kC[0:C_QK, 0, P:T], start=True, stop=True).then_inc(prep_done, 1)
                b = prep_bank(6)
                for h in range(4):
                    last = transpose(PS[:, b, h * P:(h + 1) * P], kB[:, h, 0:P])
                last.then_inc(prep_done, 1)
                sum_squares(1, sq_lora, 2, PS[:, 7, 0:T]).then_inc(ssq_ready, 1)
                gate_job(1)
                pe.wait_ge(ssq_read, l * NORMS + 2)
                pe.wait_ge(sq_ready, l * NORMS + 3)
                pe.matmul(PS[:, 7, 0:T], ones, sq_lora[:, 2, :], start=True, stop=True).then_inc(ssq_ready, 1)
                arrived(L_UQ)
                pe.wait_ge(lora_ready, l * 2 + 1)
                w = ring[:, L_UQ % RING_SLOTS, 0:2 * C_HEADS * C_QK].rearrange("p (k n) -> p k n", k=2)
                for i in range(4):
                    b = prep_bank(7 + i)
                    for h in range(2):
                        for k in range(2):
                            last = pe.matmul(PS[0:C_QK, b, h * T:(h + 1) * T], w[:, k, (2 * i + h) * C_QK:(2 * i + h + 1) * C_QK],
                                             qcn[:, k, :], start=(k == 0), stop=(k == 1))
                            if i == 0 and h == 0 and k == 0:
                                release(last)
                    last.then_inc(prep_done, 1)
                project(Z_GL + 2, L_GL)
                for i in range(2):
                    b = prep_bank(11 + i)
                    pe.wait_ge(prep_ev, l * PREP_JOBS + 9 + 2 * i)
                    pe.matmul(PS[0:C_QK, b, :], cst["swap_c"][0:C_QK, 0:C_QK], qC[0:C_QK, 4 * i:4 * i + 4, P:T],
                              start=True, stop=True).then_inc(prep_done, 1)
                pe.wait_ge(lora_ready, l * 2 + 2)
                b = prep_bank(13)
                transpose(PS[:, b, 0:P], kA[:, 0:P])
                transpose(PS[:, b, P:2 * P], ckvT[:, 0:P])
                transpose(PS[:, b, 2 * P:2 * P + C_QK], kC[0:C_QK, 0, 0:P], C_QK).then_inc(prep_done, 1)
                gate_job(3)
                for h in range(C_HEADS):
                    b = prep_bank(14 + h)
                    pe.matmul(PS[0:C_NOPE, b, 0:384], w_ukv[:, h, 0:C_NOPE], ckvT, start=True, stop=True).then_inc(prep_done, 1)
                for t in range(3):
                    b = prep_bank(22 + t)
                    pe.matmul(PS[:, b, :], ckvT[:, t * P:(t + 1) * P], w_ukv[:, :, C_NOPE:C_NOPE + C_V],
                              start=True, stop=True).then_inc(prep_done, 1)

                def scores(u):
                    br, t, g = ATT[u]
                    b = 2 + 2 * (u % 2)
                    q0, k0, kn = t * P, t * P, P + t * P
                    if u < 2:
                        pe.wait_ge(prep_ev, l * PREP_JOBS + PREP_JOBS)
                    else:
                        pe.wait_ge(prob_exp, (l * UNITS + u - 1) * 4)
                    n = 4 if t == 0 else 2
                    for i in range(n):
                        if br == "A":
                            h = n * g + i
                            kv, c = h // 4, h % 4
                            last = pe.matmul(PS[:, b, i * kn:(i + 1) * kn], qA[HD * kv:HD * (kv + 1), c, q0:q0 + P],
                                             kA[HD * kv:HD * (kv + 1), k0:k0 + kn], start=True, stop=True)
                        elif br == "B":
                            m, j = divmod(i, n // 2)
                            h = (n // 2) * g + j
                            last = pe.matmul(PS[:, b + m, j * kn:(j + 1) * kn], qB[HD * m:HD * (m + 1), h, q0:q0 + P],
                                             kB[HD * m:HD * (m + 1), h, k0:k0 + kn], start=True, stop=True)
                        else:
                            h = n * g + i
                            last = pe.matmul(PS[:, b, i * kn:(i + 1) * kn], qC[0:C_QK, h, q0:q0 + P],
                                             kC[0:C_QK, h, k0:k0 + kn], start=True, stop=True)
                    last.then_inc(scores_done, 1)

                def transposes(u):
                    br = ATT[u][0]
                    pe.wait_ge(prob_ready, l * UNITS + u + 1)
                    if u >= 1:
                        pe.wait_ge(probT_ready, l * UNITS + u)
                    for i in range(2 if br == "B" else 4):
                        last = transpose(PS[:, 6, i * P:(i + 1) * P], prob[:, u % 2, i * P:(i + 1) * P])
                    last.then_inc(prob_tr, 1)

                def weighted_values(u):
                    br, t, g = ATT[u]
                    pe.wait_ge(probT_ready, l * UNITS + u + 1)
                    if u >= 1:
                        pe.wait_ge(o_ready, l * UNITS + u)
                    heads = (2 if t == 0 else 1) if br == "B" else (4 if t == 0 else 2)
                    for i in range(heads):
                        h = heads * g + i
                        for kt in range(t + 1):
                            tile = kt + t
                            if br == "A":
                                v = vA[:, tile, (h // 4) * HD:(h // 4 + 1) * HD]
                            elif br == "B":
                                v = vB[:, tile, h * P:(h + 1) * P]
                            else:
                                v = vC[:, tile, h * C_V:(h + 1) * C_V]
                            if br == "B":
                                out = PS[:, 7, i * P:(i + 1) * P]
                            else:
                                out = PS[HD * (i % 2):HD * (i % 2) + HD, 7, (i // 2) * P:(i // 2 + 1) * P]
                            blk = i * (t + 1) + kt
                            last = pe.matmul(out, v, probT[:, u % 2, blk * P:(blk + 1) * P], start=(kt == 0), stop=(kt == t))
                    last.then_inc(pv_done, 1)

                for s in range(UNITS + 2):
                    if s < UNITS:
                        scores(s)
                    if s % 2 == 0 and s // 2 + 4 < 12:
                        gate_job(s // 2 + 4)
                    if 1 <= s <= UNITS:
                        transposes(s - 1)
                    if s >= 2:
                        weighted_values(s - 2)

                pe.wait_ge(sq_ready, l * NORMS + 4)
                for i in range(2):
                    last = pe.matmul(PS[:, 4 + i, :], ones, sq_od[:, 2 * i:2 * i + 2, :], start=True, stop=True)
                last.then_inc(ssq_ready, 1)

                pe.wait_ge(gate_ready, (l + 1) * 12)
                for j in range(KC):
                    half, jj = divmod(j, 4)
                    b = 2 * (j % 2)
                    if j >= 2:
                        pe.wait_ge(merged_ready, l * KC + j - 1)
                    for n, src in enumerate((qA, qC, qB)):
                        br = (0, 2, 1)[n]
                        if jj == 0:
                            arrived(L_BR + 3 * half + br)
                        if n == 0 and j == 0:
                            pe.wait_ge(o_ready, l * UNITS + UNITS)
                        if n == 2 and j == 0:
                            pe.wait_ge(od_ready, l + 1)
                        w = wide(L_BR + 3 * half + br)
                        for k in range(4):
                            last = pe.matmul(PS[:, b + n // 2, (n % 2) * T:(n % 2 + 1) * T], w[:, k, jj * P:(jj + 1) * P], src[:, k, :],
                                             start=(k == 0), stop=(k == 3))
                            if n == 0 and k == 0 and jj == 0:
                                release(last, 1 if half == 0 else 3)
                    last.then_inc(branch_done, 1)
                for j in range(4):
                    arrived(L_OUT + j)
                    w = slot_cols(L_OUT + j, 256)
                    for m in range(2):
                        for k in range(KC):
                            if j == 0 and m == 0:
                                pe.wait_ge(merged_ready, l * KC + k + 1)
                            last = pe.matmul(PS[:, 4 + j, m * T:(m + 1) * T], w[:, k, m * P:(m + 1) * P], merged[:, k, :],
                                             start=(k == 0), stop=(k == KC - 1))
                            if m == 0 and k == 0:
                                release(last, 3 if j == 0 else 1)
                    last.then_inc(wout_done, 1)
                sum_squares(4, sq_a, KC, PS[:, 0, 0:T]).then_inc(ssq_ready, 1)
                sum_squares(5, sq_x, KC, PS[:, 1, 0:T]).then_inc(ssq_ready, 1)

                pe.wait_ge(rw_in, (l + 1) * 16)
                pe.wait_ge(h_ready, (l * 2 * KC + 2 * KC) * 2)
                for t in range(2):
                    for k in range(KC):
                        last = pe.matmul(PS[:, 0, t * N_EXPERTS:(t + 1) * N_EXPERTS], h2T[:, k, t * P:(t + 1) * P], rw[:, k, :],
                                         start=(k == 0), stop=(k == KC - 1))
                        if t == 0 and k == 0:
                            release(last)
                last.then_inc(router_done, 1)
                arrived(L_SH)
                arrived(L_SH + 1)
                for n in range(2):
                    w = slot_cols(L_SH + n, 256)
                    for m in range(2):
                        for k in range(KC):
                            last = pe.matmul(PS[:, 6 + n, m * T:(m + 1) * T], w[:, k, m * P:(m + 1) * P], h2T[:, k, :],
                                             start=(k == 0), stop=(k == KC - 1))
                last.then_inc(shared_gu, 1)
                for j in range(4):
                    t, half = divmod(j, 2)
                    for c in range(4):
                        ch = 4 * half + c
                        last = transpose(PS[:, 2 + j, c * P:(c + 1) * P], h2T[:, ch, t * P:(t + 1) * P])
                        if j == 0 and c == 0:
                            release(last, 2)
                    last.then_inc(htok_tr, 1)
                arrived(L_SH + 2)
                pe.wait_ge(shared_hid, l + 1)
                shid = view(0, 2, T)
                w = down_slot(L_SH + 2)
                for j in range(4):
                    pe.wait_ge(htok_ready, l * 4 + j + 1)
                    for c in range(2):
                        for f in range(2):
                            last = pe.matmul(PS[:, 2 + j, c * T:(c + 1) * T], w[:, f, (2 * j + c) * P:(2 * j + c + 1) * P], shid[:, f, :],
                                             start=(f == 0), stop=(f == 1))
                    last.then_inc(shared_down, 1)
                pe.wait_ge(sel_ready, l + 1)
                release(pe.matmul(PS[:, 1, 0:64], before, sel[:, 0, :], start=True, stop=True))
                pe.matmul(PS[:, 1, 64:128], before, sel[:, 1, :], start=True, stop=False)
                pe.matmul(PS[:, 1, 64:128], ones, sel[:, 0, :], start=False, stop=True)
                pe.matmul(PS[:, 1, 128:192], ones, sel[:, 0, :], start=True, stop=False)
                pe.matmul(PS[:, 1, 128:192], ones, sel[:, 1, :], start=False, stop=True).then_inc(rank_done, 1)
                pe.wait_ge(npass_ready, l + 1)
                apart(pe)
                npass = pe.value_load(npass_i[0:1, 0:1], min_val=1, max_val=4)

                with pe.Fori(0, npass) as p:
                    q = pe.snap(before_l + p)
                    base = pe.snap(rounds + ROUNDS + p * PASS_ROUNDS)
                    for blk in range(NSB):
                        pe.wait_ge(g_ready, q * NSB + blk + 1)
                        for pair in range(2):
                            n = 2 * blk + pair
                            if n >= 2:
                                pe.wait_ge(gvt_ready, q * 2 * NSB + n - 1)
                            for i in range(2):
                                for t in range(2):
                                    c0 = (2 * pair + i) * P
                                    last = transpose(PS[:, 6 + n % 2, (2 * i + t) * P:(2 * i + t + 1) * P], gval[:, t, c0:c0 + P])
                            last.then_inc(gvt_tr, 1)
                        for c in range(KC):
                            n = KC * blk + c
                            if n == 0:
                                pe.wait_ge(y_shared, l * 4 + 4)
                            if n >= 4:
                                pe.wait_ge(xs_ready, q * NSB * KC + n - 3)
                            for t in range(2):
                                last = pe.matmul(PS[:, 2 + n % 4, :], htok[:, t, c * P:(c + 1) * P], gsel[:, t, :],
                                                 start=(t == 0), stop=(t == 1))
                            last.then_inc(gather_done, 1)
                    pe.wait_ge(xs_ready, (q + 1) * NSB * KC)
                    pe.wait_ge(off_ready, q + 1)
                    pe.wait_ge(pad_set, l + 1)
                    apart(pe)

                    def gate_up(n, off, odd, base, frees=1):
                        for half in range(2):
                            arrived(n + half, base)
                            w = slot_cols(n + half, 256)
                            for f in range(2):
                                for k in range(KC):
                                    last = pe.matmul(PS[:, odd, (2 * half + f) * CAP:(2 * half + f + 1) * CAP],
                                                     w[:, k, f * P:(f + 1) * P], xs[:, k, ds(off + CAP, CAP)],
                                                     start=(k == 0), stop=(k == KC - 1))
                                    if half == 0 and f == 0 and k == 0 and frees:
                                        release(last, frees)
                        last.then_inc(gu_done, 1)

                    def down(n, e, odd, base, frees=2, waits=True):
                        arrived(n, base)
                        pe.wait_ge(hid_ready, q * N_EXPERTS + e + 1)
                        if waits:
                            pe.wait_ge(out_ready, q * N_EXPERTS + e - 1)
                        w = down_slot(n)
                        for c in range(KC):
                            for f in range(2):
                                last = pe.matmul(PS[:, 2 + odd, c * CAP:(c + 1) * CAP], w[:, f, c * P:(c + 1) * P], hid[:, odd, f, :],
                                                 start=(f == 0), stop=(f == 1))
                                if c == 0 and f == 0:
                                    release(last, frees)
                        last.then_inc(down_done, 1)

                    def offset(e):
                        return pe.value_load(off_i[0:1, ds(e, 1)], min_val=0, max_val=SLOTS)

                    gate_up(0, offset(0), 0, base, frees=0)
                    for e in range(2):
                        gate_up(2 + 3 * e, offset(e + 1), (e + 1) % 2, base, frees=2 if e == 0 else 1)
                        down(4 + 3 * e, e, e % 2, base, waits=False)
                    with pe.Fori(0, N_EXPERTS // 4 - 1) as i:
                        for u in range(2, 6):
                            e = i * 4 + u
                            gate_up(2 + 3 * u, offset(e + 1), (u + 1) % 2, base + i)
                            down(4 + 3 * u, e, u % 2, base + i)
                    for e in range(N_EXPERTS - 2, N_EXPERTS):
                        if e < N_EXPERTS - 1:
                            gate_up(2 + 3 * e, offset(e + 1), (e + 1) % 2, base)
                            down(4 + 3 * e, e, e % 2, base)
                        else:
                            down(2 + 3 * e, e, e % 2, base, frees=1)
                    pe.wait_ge(out_ready, (q + 1) * N_EXPERTS)
                    pe.wait_ge(gvt_ready, (q + 1) * 2 * NSB)
                    for s in range(SLOTS // P + 1):
                        if s < SLOTS // P:
                            if s >= 1:
                                pe.wait_ge(otok_ready, q * 12 + s)
                            for c in range(KC):
                                last = transpose(PS[:, 4 + c // 4, (c % 4) * P:(c % 4 + 1) * P], xs[:, c, s * P:(s + 1) * P])
                                if s == 0 and c == 0:
                                    release(last)
                            last.then_inc(otok_tr, 1)
                        if s >= 1:
                            r = s - 1
                            pe.wait_ge(otok_ready, q * 12 + r + 1)
                            for c in range(KC):
                                last = pe.matmul(PS[:, c // 2, (c % 2) * T:(c % 2 + 1) * T], otok[:, r % 2, c * P:(c + 1) * P], gvalT[:, r, :],
                                                 start=(r == 0 and c % 2 == 0), stop=(r == SLOTS // P - 1), skip_group_check=True)
                            last.then_inc(comb_done, 1)
                    pe.wait_ge(y_ready, (q + 1) * 4)
                pe.reg_add(passes, passes, npass)
                sum_squares(6, view(0, KC, T), KC, PS[:, 4, 0:T]).then_inc(ssq_ready, 1)
            pe.wait_ge(x_ready, (DEPTH + 1) * XR)
            for j in range(4):
                t, half = divmod(j, 2)
                for c in range(4):
                    last = transpose(PS[:, j, c * P:(c + 1) * P], xT[:, 4 * half + c, t * P:(t + 1) * P])
                last.then_inc(end_tr, 1)

        @block.scalar
        def _(act):
            def bank(b):
                return PS[:, b, :]

            def halves(b):
                return b.rearrange("p (m t) -> p m t", m=2)

            act.wait_ge(start_tr, 5)
            act.activation(condE[:], PS[:, 4, 0:2 * KC].rearrange("p (t k) -> p k t", t=2), ACT.Exp, scale=-1.0).then_inc(cond_exp, 1)
            passes = act.alloc_register("act_passes")
            act.reg_mov(passes, 0)
            with act.Fori(0, DEPTH) as l:
                before_l = act.snap(passes, min_val=0, max_val=8)

                def squares(dst, src):
                    act.activation(dst, src, ACT.Square).then_inc(sq_ready, 1)

                def modulate(call, dst, scale, shift):
                    act.wait_ge(mod_ready, l + 1)
                    for c in range(KC):
                        act.wait_ge(hn_ready, l * 2 * KC + call * KC + c + 1)
                        for t in range(2):
                            act.activation(dst[:, c, t * P:(t + 1) * P], dst[:, c, t * P:(t + 1) * P], ACT.Identity,
                                           scale=scale[:, c, t:t + 1], bias=shift[:, c, t:t + 1]).then_inc(h_ready, 1)

                def projected(j):
                    act.wait_ge(z_done, l * Z_JOBS + j + 1)
                    return bank(j % 2)

                act.wait_ge(x_ready, (l + 1) * XR)
                squares(sq_x, xT[:])
                modulate(0, hT, pre1, modT[:, 0:KC, :])
                act.wait_ge(lam_dot, l + 1)
                act.activation(lame[:, 0:2], lame[:, 2:4], ACT.Exp).then_inc(lam_exp, 1)

                for j in range(2):
                    act.activation(qA[:, 2 * j:2 * j + 2, :], halves(projected(j)), ACT.Copy).then_inc(z_ev, 1)
                b = projected(2)
                act.activation(kA[:, 0:T], b[:, 0:T], ACT.Copy).then_inc(z_ev, 1)
                act.activation(vA[:, 0:2, :], halves(b[:, T:2 * T]), ACT.Copy).then_inc(z_ev, 1)
                for j in (3, 4):
                    act.activation(qB[:, 2 * j - 6:2 * j - 4, :], halves(projected(j)), ACT.Copy).then_inc(z_ev, 1)
                for j in (5, 6):
                    act.activation(kB[:, 2 * j - 10:2 * j - 8, 0:T], halves(projected(j)), ACT.Copy).then_inc(z_ev, 1)
                for j in (7, 8):
                    act.activation(vB[:, 0:2, (j - 7) * T:(j - 6) * T], halves(projected(j)), ACT.Copy).then_inc(z_ev, 1)
                act.activation(qcT, halves(projected(Z_QC)), ACT.Copy).then_inc(z_ev, 1)
                b = projected(Z_KVC)
                act.activation(kvcT, b[:, 0:T], ACT.Copy).then_inc(z_ev, 1)
                act.activation(kC[0:C_QK, 0, 0:T], b[0:C_QK, T:2 * T], ACT.Copy).then_inc(z_ev, 1)
                act.wait_ge(z_ev, l * projections_out(Z_JOBS - 1) + projections_out(Z_KVC))
                squares(sq_lora[:, 0:2, :], qcT)
                squares(sq_lora[:, 2, :], kvcT)

                def gate_exp(g):
                    act.activation(gates[:, 2 * g:2 * g + 2, :], halves(projected(Z_GL + g)), ACT.Exp, scale=-1.0).then_inc(z_ev, 1)

                for g in range(4):
                    gate_exp(g)

                def exponentiate(u):
                    br, t, g = ATT[u]
                    act.wait_ge(negm_ready, l * UNITS + u + 1)
                    b = 2 + 2 * (u % 2)
                    n, kn = (4, P) if t == 0 else (2, 2 * P)
                    if u >= 2:
                        act.wait_ge(prob_tr, l * UNITS + u - 1)
                    if br == "A":
                        act.activation(sinke[:, u % 2, 0:n], sinke[:, u % 2, 0:n], ACT.Exp).then_inc(sink_exp, 1)
                    for i in range(n):
                        m, j = divmod(i, n // 2)
                        src = PS[:, b + m, j * kn:(j + 1) * kn] if br == "B" else PS[:, b, i * kn:(i + 1) * kn]
                        act.activation(prob[:, u % 2, i * kn:(i + 1) * kn], src, ACT.Exp,
                                       scale=(C_QK if br == "C" else HD) ** -0.5, bias=negm[:, u % 2, i:i + 1],
                                       accum_out=psums[:, u % 2, i:i + 1]).then_inc(prob_exp, 4 // n)

                def copy_probT(u):
                    n = 2 if ATT[u][0] == "B" else 4
                    act.wait_ge(prob_tr, l * UNITS + u + 1)
                    if u >= 2:
                        act.wait_ge(pv_done, l * UNITS + u - 1)
                    act.activation(probT[:, u % 2, 0:n * P], PS[:, 6, 0:n * P], ACT.Copy).then_inc(probT_ready, 1)

                act.wait_ge(prep_ev, l * PREP_JOBS + PREP_JOBS)
                for s in range(UNITS + 1):
                    if s < UNITS:
                        exponentiate(s)
                    if s % 2 == 0 and s // 2 + 4 < 12:
                        gate_exp(s // 2 + 4)
                    if s >= 1:
                        copy_probT(s - 1)
                act.wait_ge(o_ready, l * UNITS + 12)
                squares(sq_od, qB)

                act.wait_ge(state_out, (l + 1) * 6 * 16)
                for j in range(4):
                    act.wait_ge(wout_done, l * 4 + j + 1)
                    act.activation(aT[:, 2 * j:2 * j + 2, :], halves(bank(4 + j)), ACT.Copy).then_inc(a_ready, 1)
                act.wait_ge(a_ready, l * 4 + 4)
                squares(sq_a, aT)
                act.wait_ge(x1_ready, (l + 1) * 2 * KC)
                squares(sq_x, xT[:])
                modulate(1, h2T, pre2, modT[:, 24:32, :])

                act.wait_ge(router_done, l + 1)
                act.activation(r_score, bank(0)[:, 0:2 * N_EXPERTS].rearrange("p (t e) -> p t e", t=2), ACT.Exp, scale=-1.0).then_inc(route_exp, 1)
                act.wait_ge(shared_gu, l + 1)
                act.activation(ssig, halves(bank(6)), ACT.Exp, scale=-1.0).then_inc(shared_exp, 1)
                for j in range(4):
                    t, half = divmod(j, 2)
                    act.wait_ge(htok_tr, l * 4 + j + 1)
                    act.activation(htok[:, t, half * 512:(half + 1) * 512], bank(2 + j), ACT.Copy).then_inc(htok_ready, 1)
                for j in range(4):
                    act.wait_ge(shared_down, l * 4 + j + 1)
                    act.activation(yT[:, 2 * j:2 * j + 2, :], halves(bank(2 + j)), ACT.Copy).then_inc(y_shared, 1)
                act.wait_ge(npass_ready, l + 1)
                apart(act)
                npass = act.value_load(npass_i[0:1, 0:1], min_val=1, max_val=4)
                with act.Fori(0, npass) as p:
                    q = act.snap(before_l + p)
                    for blk in range(NSB):
                        for pair in range(2):
                            n = 2 * blk + pair
                            act.wait_ge(gvt_tr, q * 2 * NSB + n + 1)
                            act.activation(gvalT[:, 4 * blk + 2 * pair:4 * blk + 2 * pair + 2, :], halves(bank(6 + n % 2)), ACT.Copy).then_inc(gvt_ready, 1)
                        for c in range(KC):
                            n = KC * blk + c
                            act.wait_ge(gather_done, q * NSB * KC + n + 1)
                            act.activation(xs[:, c, CAP + blk * SB:CAP + (blk + 1) * SB], bank(2 + n % 4), ACT.Copy).then_inc(xs_ready, 1)
                    act.wait_ge(off_ready, q + 1)
                    act.wait_ge(xs_ready, (q + 1) * NSB * KC)

                    def sigmoid_exp(e, odd, waits=True):
                        act.wait_ge(gu_done, q * N_EXPERTS + e + 1)
                        if waits:
                            act.wait_ge(hid_ready, q * N_EXPERTS + e - 1)
                        act.activation(sig[:, odd, :], PS[:, odd, 0:2 * CAP], ACT.Exp, scale=-1.0).then_inc(sig_ready, 1)

                    def put_out(e, odd, waits=True):
                        off = act.value_load(off_i[0:1, ds(e, 1)], min_val=0, max_val=SLOTS)
                        act.wait_ge(down_done, q * N_EXPERTS + e + 1)
                        if waits:
                            act.wait_ge(out_ready, q * N_EXPERTS + e)
                        act.activation(xs[:, :, ds(off, CAP)], PS[:, 2 + odd, :].rearrange("p (c s) -> p c s", c=KC), ACT.Copy).then_inc(out_ready, 1)

                    sigmoid_exp(0, 0, waits=False)
                    sigmoid_exp(1, 1, waits=False)
                    put_out(0, 0, waits=False)
                    with act.Fori(0, N_EXPERTS // 2 - 1) as i:
                        for u in range(2):
                            e = i * 2 + u
                            sigmoid_exp(e + 2, u)
                            put_out(e + 1, 1 - u)
                    put_out(N_EXPERTS - 1, 1)
                    for s in range(SLOTS // P):
                        act.wait_ge(otok_tr, q * 12 + s + 1)
                        if s >= 2:
                            act.wait_ge(comb_done, q * 12 + s - 1)
                        act.activation(otok[:, s % 2, :], PS[:, 4:6, :].rearrange("p a b -> p (a b)"), ACT.Copy).then_inc(otok_ready, 1)
                act.wait_ge(y_ready, (before_l + npass) * 4)
                squares(view(0, KC, T), yT)
                act.reg_add(passes, passes, npass)
            for j in range(4):
                t, half = divmod(j, 2)
                act.wait_ge(end_tr, j + 1)
                act.activation(view(0, 2, D)[:, t, half * 512:(half + 1) * 512], bank(j), ACT.Copy).then_inc(end_ev, 1)

        @block.vector
        def _(dve):
            ve = nc.vector

            class Chain:

                def __init__(self, semaphore, base):
                    self.semaphore, self.base, self.n = semaphore, base, 0

                def __call__(self, ins, own=False):
                    self.add(ins)
                    dve.wait_ge(self.semaphore, self.base + self.n)
                    if own:
                        apart(dve)

                def add(self, ins):
                    self.n += 1
                    ins.then_inc(self.semaphore, 1)

            start = Chain(start_step, 0)
            for j in range(4):
                dve.wait_ge(start_tr, j + 1)
                ve.tensor_copy(xT[:, 2 * j:2 * j + 2, :], PS[:, j, :].rearrange("p (c t) -> p c t", c=2)).then_inc(x_ready, XR // 4)
            dve.wait_ge(cond_exp, 1)
            start(ve.tensor_scalar(condE[:], condE[:], 1.0, None, ALU.add))
            start(ve.reciprocal(condE[:], condE[:]))
            dve.wait_ge(start_tr, 5)
            ve.tensor_tensor(condT[:], PS[:, 4, 0:2 * KC].rearrange("p (t k) -> p k t", t=2), condE[:], ALU.mult).then_inc(cond_ready, 1)

            passes = dve.alloc_register("dve_passes")
            dve.reg_mov(passes, 0)
            with dve.Fori(0, DEPTH) as l:
                before_l = dve.snap(passes, min_val=0, max_val=8)
                step = Chain(vector_step, l * VECTOR_STEPS)

                def per_column(v, shape, axis):
                    return v.unsqueeze(axis).broadcast_to(shape)

                def rstd(n, src, channels, scratch):
                    var, y, t = scratch
                    dve.wait_ge(ssq_ready, l * NORMS + n + 1)
                    ve.tensor_scalar(var, src, 1.0 / channels, EPS, ALU.mult, ALU.add).then_inc(ssq_read, 1)
                    dve.wait_ge(ssq_read, l * NORMS + n + 1)
                    step(ve.tensor_scalar(t.bitcast(I32), var.bitcast(I32), 1, None, ALU.arith_shift_right))
                    step(ve.tensor_scalar(y.bitcast(I32), t.bitcast(I32), -1.0, float(0x5F3759DF), ALU.mult, ALU.add))
                    for _ in range(3):
                        step(ve.scalar_tensor_tensor(out=t, in0=y, scalar=-0.5, in1=y, op0=ALU.mult, op1=ALU.mult))
                        step(ve.tensor_tensor(t, t, var, ALU.mult))
                        step(ve.scalar_tensor_tensor(out=y, in0=t, scalar=1.5, in1=y, op0=ALU.add, op1=ALU.mult))
                    return y

                def normalise_x(n, dst, src, scratch):
                    r = rstd(n, src, D, scratch)
                    for c in range(KC):
                        ve.tensor_tensor(dst[:, c, :], xT[:, c, :], r, ALU.mult).then_inc(hn_ready, 1)

                def add_normalised(n, a_, src, post, scratch, done):
                    r = rstd(n, src, D, scratch)
                    step(ve.tensor_tensor(a_, a_, per_column(r, [P, KC, T], 1), ALU.mult))
                    for c in range(KC):
                        for t in range(2):
                            xs_ = xT[:, c, t * P:(t + 1) * P]
                            ve.scalar_tensor_tensor(out=xs_, in0=a_[:, c, t * P:(t + 1) * P], scalar=post[:, c, t:t + 1], in1=xs_,
                                                    op0=ALU.mult, op1=ALU.add).then_inc(done, 1)

                dve.wait_ge(x_ready, (l + 1) * XR)
                normalise_x(0, hT, PS[:, 0, 0:T], norm_scratch(21760, T))
                dve.wait_ge(params_tr, l + 1)
                step(ve.tensor_copy(parT[:], PS[:, 6, 0:84]))
                dve.wait_ge(params_in, (l + 1) * 11 * 16)
                step(ve.tensor_scalar(nsink[:], sink[:], -1.0, None, ALU.mult))
                step(ve.tensor_scalar(subl[:], parT[:, 83:84], lamc[:, 1:2], None, ALU.mult))

                def prep(i):
                    dve.wait_ge(prep_done, l * PREP_JOBS + i + 1)
                    return PS[:, 2 + i % 5, :]

                b = prep(0)
                ve.tensor_copy(kB[:, :, T:T + P], b.rearrange("p (h s) -> p h s", h=4)).then_inc(prep_ev, 1)
                b = prep(1)
                step(ve.tensor_copy(kA[:, T:T + P], b[:, 0:P]))
                step(ve.tensor_copy(ckvT[:, T:T + P], b[:, P:2 * P]))
                ve.tensor_copy(kC[C_NOPE:C_QK, :, T:T + P], per_column(b[C_NOPE:C_QK, 2 * P:3 * P], [C_ROPE, C_HEADS, P], 1)).then_inc(prep_ev, 1)
                dve.wait_ge(lam_loaded, (l + 1) * 4 * 16)
                step(ve.tensor_tensor(lam_t, lam_in[:, 0:2, :], lam_in[:, 2:4, :], ALU.mult))
                ve.reduce_sum(lame[:, 2:4], lam_t, X).then_inc(lam_dot, 1)
                dve.wait_ge(mod_done, l + 1)

                def gain(c0, n=KC):
                    return per_column(parT[:, c0:c0 + n], [P, n, 2], 2)

                step(ve.tensor_tensor(modT[:], PS[:, 7, 0:96].rearrange("p (m t) -> p m t", t=2), gain(0, 48), ALU.add))
                for dst, m, g in ((pre1, 8, 48), (pre2, 32, 64)):
                    step(ve.scalar_tensor_tensor(out=dst[:], in0=modT[:, m:m + KC, :], scalar=1.0, in1=gain(g), op0=ALU.add, op1=ALU.mult))
                step(ve.tensor_tensor(post2[:], modT[:, 40:48, :], gain(72), ALU.mult))
                ve.tensor_tensor(post1[:], modT[:, 16:24, :], gain(56), ALU.mult).then_inc(mod_ready, 1)
                dve.wait_ge(lam_exp, l + 1)
                step(ve.tensor_tensor(lame[:, 2:3], lame[:, 1:2], lame[:, 0:1], ALU.subtract))
                step(ve.tensor_tensor(lame[:, 3:4], lame[:, 2:3], lamc[:, 0:1], ALU.subtract))

                def rotate(dst, swapped, cos, sin, tmp):
                    step(ve.tensor_tensor(tmp, swapped, sin, ALU.mult))
                    step(ve.tensor_tensor(dst, dst, cos, ALU.mult))
                    return ve.tensor_tensor(dst, dst, tmp, ALU.add)

                rope4 = rope_t.rearrange("p (h s) -> p h s", h=4)
                for i, dst in ((2, qA), (3, qB), (4, kB)):
                    b = prep(i).rearrange("p (h s) -> p h s", h=4)
                    rotate(dst[:, :, P:T], b, per_column(cst["cos_ab"], [P, 4, P], 1), per_column(cst["sin_ab"], [P, 4, P], 1), rope4).then_inc(prep_ev, 1)
                    dve.wait_ge(prep_ev, l * PREP_JOBS + i + 1)
                b = prep(5)
                step(rotate(kA[:, P:T], b[:, 0:P], cst["cos_ab"], cst["sin_ab"], rope_t[:, 0:P]))
                rk = slice(C_NOPE, C_QK)
                step(rotate(kC[rk, 0, P:T], b[rk, P:T], cst["cos_c"][rk, :], cst["sin_c"][rk, :], rope_t[rk, P:T]))
                ve.tensor_copy(kC[rk, 1:C_HEADS, 0:T], kC[rk, 0:1, 0:T].broadcast_to([C_ROPE, C_HEADS - 1, T])).then_inc(prep_ev, 1)
                b = prep(6)
                ve.tensor_copy(state[:, 0:512], b).then_inc(prep_ev, 1)
                r = rstd(1, PS[:, 7, 0:T], Q_LORA, norm_scratch(19968, T))
                step(ve.scalar_tensor_tensor(out=qcn[:, 0, :], in0=qcT[:, 0, :], scalar=parT[:, 80:81], in1=r, op0=ALU.mult, op1=ALU.mult))
                ve.scalar_tensor_tensor(out=qcn[:, 1, :], in0=qcT[:, 1, :], scalar=parT[:, 81:82], in1=r, op0=ALU.mult, op1=ALU.mult).then_inc(lora_ready, 1)
                dve.wait_ge(lora_ready, l * 2 + 1)
                r = rstd(2, PS[:, 7, 0:T], KV_LORA, norm_scratch(19968, T))
                ve.scalar_tensor_tensor(out=ckvT[:, 0:T], in0=kvcT, scalar=parT[:, 82:83], in1=r, op0=ALU.mult, op1=ALU.mult).then_inc(lora_ready, 1)
                for i in range(4):
                    b = prep(7 + i)
                    ve.tensor_copy(qC[0:C_QK, 2 * i:2 * i + 2, :], b[0:C_QK, :].rearrange("p (h t) -> p h t", h=2)).then_inc(prep_ev, 1)
                dve.wait_ge(prep_ev, l * PREP_JOBS + 11)
                qk = slice(0, C_QK)
                for i in range(2):
                    b = prep(11 + i)[qk].rearrange("p (h s) -> p h s", h=4)
                    rotate(qC[qk, 4 * i:4 * i + 4, P:T], b, per_column(cst["cos_c"][qk, :], [C_QK, 4, P], 1),
                           per_column(cst["sin_c"][qk, :], [C_QK, 4, P], 1), rope4[qk]).then_inc(prep_ev, 1)
                    dve.wait_ge(prep_ev, l * PREP_JOBS + 12 + i)
                b = prep(13)
                step(ve.tensor_copy(state[:, 512:768], b[:, 0:2 * P]))
                ve.tensor_copy(state[:, 768:800], b[:, 2 * P + C_NOPE:2 * P + C_QK]).then_inc(prep_ev, 1)
                for h in range(C_HEADS):
                    b = prep(14 + h)
                    ve.tensor_copy(kC[0:C_NOPE, h, :], b[0:C_NOPE, 0:384]).then_inc(prep_ev, 1)
                for t in range(3):
                    b = prep(22 + t)
                    ve.tensor_copy(vC[:, t, :], b).then_inc(prep_ev, 1)

                def finish_gate(g):
                    dve.wait_ge(z_ev, l * projections_out(Z_JOBS - 1) + projections_out(Z_GL + g))
                    v = gates[:, 2 * g:2 * g + 2, :]
                    step(ve.tensor_scalar(v, v, 1.0, None, ALU.add))
                    ve.reciprocal(v, v).then_inc(gate_ready, 1)

                for g in range(4):
                    finish_gate(g)

                def row_maxima(u):
                    br, t, g = ATT[u]
                    dve.wait_ge(scores_done, l * UNITS + u + 1)
                    b = 2 + 2 * (u % 2)
                    n, kn = (4, P) if t == 0 else (2, 2 * P)
                    scale = (C_QK if br == "C" else HD) ** -0.5
                    m = negm[:, u % 2, 0:n]
                    if br == "B":
                        s = PS[:, b:b + 2, 0:(n // 2) * kn].rearrange("p m (j k) -> p m j k", k=kn)
                        step(ve.reduce_max(m.rearrange("p (m j) -> p m j", m=2), s, X))
                    else:
                        step(ve.reduce_max(m, PS[:, b, :].rearrange("p (i k) -> p i k", k=kn), X))
                    if br == "A":
                        ns = nsink[:, n * g:n * g + n]
                        step(ve.scalar_tensor_tensor(out=m, in0=m, scalar=-scale, in1=ns, op0=ALU.mult, op1=ALU.min))
                        ve.tensor_tensor(sinke[:, u % 2, 0:n], m, ns, ALU.subtract).then_inc(negm_ready, 1)
                    else:
                        ve.tensor_scalar(m, m, -scale, None, ALU.mult).then_inc(negm_ready, 1)

                def normalise(u):
                    br, t, g = ATT[u]
                    n, kn = (4, P) if t == 0 else (2, 2 * P)
                    dve.wait_ge(prob_exp, (l * UNITS + u + 1) * 4)
                    s, r = psums[:, u % 2, 0:n], prec[:, u % 2, 0:n]
                    if br == "A":
                        dve.wait_ge(sink_exp, l * 6 + u + 1)
                        step(ve.tensor_tensor(s, s, sinke[:, u % 2, 0:n], ALU.add))
                    step(ve.reciprocal(r, s))
                    if br == "B":
                        step(ve.tensor_scalar(r[:, n // 2:n], r[:, n // 2:n], lame[:, 3:4], None, ALU.mult))
                    pr = prob[:, u % 2, :].rearrange("p (i k) -> p i k", k=kn)
                    ins = ve.tensor_tensor(pr, pr, per_column(r, [P, n, kn], 2), ALU.mult)
                    if br == "B":
                        step(ins)
                        ins = ve.tensor_tensor(prob[:, u % 2, 0:T], prob[:, u % 2, 0:T], prob[:, u % 2, T:2 * T], ALU.add)
                    ins.then_inc(prob_ready, 1)

                def heads_out(u):
                    br, t, g = ATT[u]
                    dve.wait_ge(pv_done, l * UNITS + u + 1)
                    q_ = {"A": qA, "B": qB, "C": qC}[br]
                    if t == 0:
                        ins = ve.tensor_copy(q_[:, 2 * g:2 * g + 2, 0:P], PS[:, 7, 0:T].rearrange("p (h s) -> p h s", h=2))
                    else:
                        ins = ve.tensor_copy(q_[:, g, P:T], PS[:, 7, 0:P])
                    ins.then_inc(o_ready, 1)

                for s in range(UNITS + 3):
                    if s < UNITS:
                        row_maxima(s)
                    if s >= 3:
                        heads_out(s - 3)
                    if 1 <= s <= UNITS:
                        normalise(s - 1)
                    if s % 2 == 1 and s // 2 + 4 < 12:
                        finish_gate(s // 2 + 4)

                r = rstd(3, PS[:, 4:6, :].rearrange("p a b -> p (a b)"), P, norm_scratch(12288, 4 * T))
                ve.scalar_tensor_tensor(out=qB, in0=qB, scalar=subl[:, 0:1], in1=r.rearrange("p (h t) -> p h t", h=4),
                                        op0=ALU.mult, op1=ALU.mult).then_inc(od_ready, 1)
                dve.wait_ge(od_ready, l + 1)
                for j in range(KC):
                    dve.wait_ge(branch_done, l * KC + j + 1)
                    b = 2 * (j % 2)
                    m = merged[:, j, :]
                    step(ve.tensor_tensor(m, PS[:, b, 0:T], gates[:, j, :], ALU.mult))
                    step(ve.tensor_tensor(merge_t[:, 0, :], PS[:, b, T:2 * T], gates[:, 16 + j, :], ALU.mult))
                    step(ve.tensor_tensor(merge_t[:, 1, :], PS[:, b + 1, 0:T], gates[:, 8 + j, :], ALU.mult))
                    step(ve.tensor_tensor(m, m, merge_t[:, 0, :], ALU.add))
                    ve.tensor_tensor(m, m, merge_t[:, 1, :], ALU.add).then_inc(merged_ready, 1)
                    dve.wait_ge(merged_ready, l * KC + j + 1)
                add_normalised(4, aT, PS[:, 0, 0:T], post1, norm_scratch(8192, T), x1_ready)
                dve.wait_ge(x1_ready, (l + 1) * 2 * KC)
                normalise_x(5, h2T, PS[:, 1, 0:T], norm_scratch(8192, T))

                both = [P, 2, N_EXPERTS]
                FAR = 3.0e38
                for v in (r_gs[:, :, 8:12], r_mask[:, :, N_EXPERTS:N_EXPERTS + 2]):
                    step(ve.memset(v, -FAR))
                dve.wait_ge(route_exp, l + 1)
                step(ve.tensor_scalar(r_score, r_score, 1.0, None, ALU.add))
                step(ve.reciprocal(r_score, r_score))
                step(ve.tensor_tensor(r_bias, r_score, per_column(rbias[:], both, 1), ALU.add), own=True)
                for t in range(2):
                    for g in range(N_GROUPS):
                        step.add(ve.max(r_top[:, t * N_GROUPS + g, :], r_bias[:, t, 8 * g:8 * g + 8]))
                dve.wait_ge(vector_step, step.base + step.n)
                tops = r_top.rearrange("p (t g) k -> p t g k", t=2)
                step(ve.tensor_tensor(r_gs[:, :, 0:8], tops[:, :, :, 0], tops[:, :, :, 1], ALU.add), own=True)
                for t in range(2):
                    step.add(ve.max(r_g8[:, t, :], r_gs[:, t, 0:8]))
                dve.wait_ge(vector_step, step.base + step.n)
                step(ve.memset(r_g8[:, :, TOPK_GROUPS:8], -FAR), own=True)
                for t in range(2):
                    step.add(ve.match_replace(out=r_grep[:, t, :], in_to_replace=r_g8[:, t, :], in_values=r_gs[:, t, :], imm_value=FAR))
                dve.wait_ge(vector_step, step.base + step.n)
                step(ve.tensor_scalar(r_gm, r_grep[:, :, 0:8], FAR / 2, None, ALU.is_ge))
                grouped = [P, 2, N_GROUPS, 8]
                for t in range(2):
                    step(ve.tensor_tensor(r_mask[:, t, 0:N_EXPERTS].rearrange("p (g k) -> p g k", g=8), r_bias[:, t, :].rearrange("p (g k) -> p g k", g=8),
                                          per_column(r_gm[:, t, :], grouped[0:1] + grouped[2:], 2), ALU.mult))
                step(ve.tensor_scalar(r_gm, r_gm, 1e30, -1e30, ALU.mult, ALU.add))
                for t in range(2):
                    v = r_mask[:, t, 0:N_EXPERTS].rearrange("p (g k) -> p g k", g=8)
                    step(ve.tensor_tensor(v, v, per_column(r_gm[:, t, :], grouped[0:1] + grouped[2:], 2), ALU.add), own=True)
                for t in range(2):
                    step.add(ve.max(r_m8[:, t, :], r_mask[:, t, 0:N_EXPERTS]))
                dve.wait_ge(vector_step, step.base + step.n)
                step(ve.memset(r_m8[:, :, TOP_K:8], -FAR), own=True)
                for t in range(2):
                    step.add(ve.match_replace(out=r_mrep[:, t, :], in_to_replace=r_m8[:, t, :], in_values=r_mask[:, t, :], imm_value=FAR))
                dve.wait_ge(vector_step, step.base + step.n)
                ve.tensor_scalar(sel[:], r_mrep[:, :, 0:N_EXPERTS], FAR / 2, None, ALU.is_ge).then_inc(sel_ready, 1)
                dve.wait_ge(sel_ready, l + 1)
                step(ve.tensor_tensor(gatew[:], r_score, sel[:], ALU.mult))
                step(ve.reduce_sum(r_sum, gatew[:], X))
                step(ve.reciprocal(r_sum, r_sum))
                step(ve.tensor_scalar(r_sum, r_sum, ROUTED_SCALE, None, ALU.mult))
                step(ve.tensor_tensor(gatew[:], gatew[:], per_column(r_sum, both, 2), ALU.mult))

                dve.wait_ge(shared_exp, l + 1)
                dve.wait_ge(shared_gu, l + 1)
                step(ve.tensor_scalar(ssig, ssig, 1.0, None, ALU.add))
                step(ve.reciprocal(ssig, ssig))
                step(ve.tensor_tensor(ssig, PS[:, 6, :].rearrange("p (f t) -> p f t", f=2), ssig, ALU.mult))
                ve.tensor_tensor(view(0, 2, T), PS[:, 7, :].rearrange("p (f t) -> p f t", f=2), ssig, ALU.mult).then_inc(shared_hid, 1)

                dve.wait_ge(rank_done, l + 1)
                step(ve.tensor_copy(rank[:], PS[:, 1, 0:128].rearrange("p (t e) -> p t e", t=2)))
                step(ve.tensor_copy(count[:], PS[:, 1, 128:192]))
                step(ve.reduce_max(r_most, count[:], X))
                step(ve.tensor_scalar(r_np, r_most, CAP + 0.5, 1.0, ALU.is_gt, ALU.add))
                for k in (2, 3):
                    step(ve.scalar_tensor_tensor(out=r_np, in0=r_most, scalar=k * CAP + 0.5, in1=r_np, op0=ALU.is_gt, op1=ALU.add))
                ve.tensor_copy(npass_i[:], r_np).then_inc(npass_ready, 1)
                ve.memset(xs[:, :, CAP + SLOTS:XSW], 0.0).then_inc(pad_set, 1)
                dve.wait_ge(state_out, (l + 1) * 6 * 16)
                step(ve.memset(r_scan[:, :, 0:33], 0.0))
                dve.wait_ge(npass_ready, l + 1)
                apart(dve)
                npass = dve.value_load(npass_i[0:1, 0:1], min_val=1, max_val=4)
                assert step.n == VECTOR_STEPS, step.n

                with dve.Fori(0, npass) as p:
                    q = dve.snap(before_l + p)
                    pstep = Chain(pass_step, q * PASS_STEPS)
                    pstep(ve.scalar_tensor_tensor(out=r_selp, in0=rank[:], scalar=0.0, in1=sel[:], op0=ALU.is_ge, op1=ALU.mult))
                    pstep(ve.scalar_tensor_tensor(out=r_selp, in0=rank[:], scalar=CAP - 0.5, in1=r_selp, op0=ALU.is_lt, op1=ALU.mult))
                    pstep(ve.tensor_scalar(r_cnt, count[:], 0.0, float(CAP), ALU.max, ALU.min))
                    pstep(ve.tensor_copy(r_scan[:, 0, 33:96], r_cnt[:, 0:63]))
                    for k in range(6):
                        s, d = k % 2, 1 - k % 2
                        pstep(ve.tensor_tensor(r_scan[:, d, 32:96], r_scan[:, s, 32:96], r_scan[:, s, 32 - 2 ** k:96 - 2 ** k], ALU.add))
                    off = r_scan[:, 0, 32:96]
                    ve.tensor_copy(off_i[:], off).then_inc(off_ready, 1)
                    pstep(ve.tensor_tensor(r_val, rank[:], per_column(off, both, 1), ALU.add))
                    pstep(ve.scalar_tensor_tensor(out=r_val, in0=r_val, scalar=1.0, in1=r_selp, op0=ALU.add, op1=ALU.mult))
                    pstep(ve.tensor_scalar(r_val, r_val, -1.0, None, ALU.add))
                    pstep(ve.tensor_tensor(r_gwp, gatew[:], r_selp, ALU.mult), own=True)
                    for t in range(2):
                        pstep.add(ve.max(r_pos[:, t, :], r_val[:, t, :]))
                    dve.wait_ge(pass_step, pstep.base + pstep.n)
                    for t in range(2):
                        for k in range(TOP_K):
                            pstep(ve.scalar_tensor_tensor(out=r_junk, in0=r_val[:, t, :], scalar=r_pos[:, t, k:k + 1], in1=r_gwp[:, t, :],
                                                          op0=ALU.is_equal, op1=ALU.mult, accum_out=r_wk[:, t, k:k + 1]))
                    for blk in range(NSB):
                        if blk:
                            pstep(ve.tensor_scalar(r_pos, r_pos, -float(SB), None, ALU.add))
                            dve.wait_ge(gather_done, q * NSB * KC + KC * blk)
                        for t in range(2):
                            pstep(ve.tensor_scalar(gval[:, t, :], iota, r_pos[:, t, 0:1], r_wk[:, t, 0:1], ALU.is_equal, ALU.mult))
                            for k in range(1, TOP_K):
                                pstep(ve.tensor_scalar(r_tmp, iota, r_pos[:, t, k:k + 1], r_wk[:, t, k:k + 1], ALU.is_equal, ALU.mult))
                                pstep(ve.tensor_tensor(gval[:, t, :], gval[:, t, :], r_tmp, ALU.add))
                        ve.tensor_scalar(gsel, gval, 0.0, None, ALU.is_gt).then_inc(g_ready, 1)
                    pstep(ve.tensor_scalar(rank[:], rank[:], -float(CAP), None, ALU.add))
                    pstep(ve.tensor_scalar(count[:], count[:], -float(CAP), None, ALU.add))
                    assert pstep.n == PASS_STEPS, pstep.n

                    def hidden(e, odd, waits=True):
                        chain = Chain(expert_step, (q * N_EXPERTS + e) * 3)
                        dve.wait_ge(sig_ready, q * N_EXPERTS + e + 1)
                        s = sig[:, odd, :]
                        chain(ve.tensor_scalar(s, s, 1.0, None, ALU.add))
                        chain(ve.reciprocal(s, s))
                        chain(ve.tensor_tensor(act_g, PS[:, odd, 0:2 * CAP], s, ALU.mult))
                        if waits:
                            dve.wait_ge(down_done, q * N_EXPERTS + e - 1)
                        ve.tensor_tensor(hid[:, odd, :, :].rearrange("p f s -> p (f s)"), PS[:, odd, 2 * CAP:4 * CAP], act_g, ALU.mult).then_inc(hid_ready, 1)

                    for e in range(2):
                        hidden(e, e, waits=False)
                    with dve.Fori(0, N_EXPERTS // 2 - 1) as i:
                        for u in range(2):
                            hidden(i * 2 + (2 + u), u)
                    dve.wait_ge(y_shared, l * 4 + 4)
                    dve.wait_ge(comb_done, (q + 1) * 12)
                    for j in range(4):
                        v = yT[:, 2 * j:2 * j + 2, :]
                        ve.tensor_tensor(v, v, PS[:, j, :].rearrange("p (c t) -> p c t", c=2), ALU.add).then_inc(y_ready, 1)
                    dve.wait_ge(y_ready, (q + 1) * 4)
                dve.reg_add(passes, passes, npass)
                step = Chain(tail_step, l * TAIL_STEPS)
                add_normalised(6, yT, PS[:, 4, 0:T], post2, norm_scratch(15360, T), x_ready)
                assert step.n == TAIL_STEPS, step.n


_INS = ["x_prompt", "x_sample", "cache_swa_k", "cache_swa_v", "cache_dif_k", "cache_dif_v", "cache_mla_ckv",
        "cache_mla_kpe", "c", "c_ctx", "w_mod", "b_mod", "norm_attn_pre", "norm_attn_post", "norm_ffn_pre",
        "norm_ffn_post", "w_in", "swa_sink", "dif_lq1", "dif_lk1", "dif_lq2", "dif_lk2", "dif_subln", "mla_q_norm",
        "mla_w_uq", "mla_kv_norm", "mla_w_ukv", "w_branch_a", "w_branch_b", "w_branch_c", "w_out", "router_w",
        "router_bias", "moe_w_gate", "moe_w_up", "moe_w_down", "shared_w_gate", "shared_w_up", "shared_w_down"]
_OUTS = {"y_prompt": (1, P, D), "y_sample": (1, P, D), "swa_k": (1, DEPTH, P, A_KV, HD), "swa_v": (1, DEPTH, P, A_KV, HD),
         "dif_k": (1, DEPTH, P, B_HEADS, 2, HD), "dif_v": (1, DEPTH, P, B_HEADS, 2 * HD), "ckv": (1, DEPTH, P, KV_LORA),
         "kpe": (1, DEPTH, P, C_ROPE)}


def kernel(**inputs):
    import concourse.bacc as bacc
    from concourse.bass_utils import run_bass_kernel_spmd

    nc = bacc.Bacc("TRN2", target_bir_lowering=False, num_devices=1)
    tables, lams = constants()
    arrays = {name: np.ascontiguousarray(inputs[name]) for name in _INS}
    arrays["consts"], arrays["lam_consts"] = tables, lams
    ins = {name: nc.dram_tensor(f"in_{name}", v.shape, mybir.dt.from_np(v.dtype), kind="ExternalInput").ap()
           for name, v in arrays.items()}
    outs = {name: nc.dram_tensor(f"out_{name}", shape, F32, kind="ExternalOutput").ap() for name, shape in _OUTS.items()}
    hybrid_layers(nc, ins, outs)
    r = run_bass_kernel_spmd(nc, [{f"in_{name}": v for name, v in arrays.items()}], core_ids=[0])
    return tuple(r.results[0][f"out_{name}"] for name in _OUTS)
```

```python
import math
from contextlib import ExitStack

import numpy as np

import concourse.bass as bass
from concourse import mybir
from concourse.bass import ds

F32 = mybir.dt.float32
I32 = mybir.dt.int32
ALU = mybir.AluOpType
ACT = mybir.ActivationFunctionType
X = mybir.AxisListType.X

P = 128
D = 1024
KC = D // P
T = 256
DEPTH = 2
GRID_W = 64
ROPE_BASE = 10000.0
EPS = 1e-6
A_HEADS, A_KV, HD = 8, 2, 64
B_HEADS = 4
C_HEADS, C_NOPE, C_ROPE, C_V = 8, 64, 32, 64
C_QK = C_NOPE + C_ROPE
Q_LORA, KV_LORA = 256, 128
N_EXPERTS, N_GROUPS, TOP_K, TOPK_GROUPS, F_EXPERT = 64, 8, 6, 4, 256
ROUTED_SCALE = 2.5
CAP = 64
SLOTS = T * TOP_K
SB = 512
NSB = SLOTS // SB
XSW = CAP + SLOTS + CAP

QA, KA, VA = 0, 512, 640
QD, KD, VD = 768, 1280, 1792
QC, KVC, KPE, GL = 2304, 2560, 2688, 2720

RING_SLOTS = 12
LOADS = 60
EXPERT_LOADS = 3 * N_EXPERTS
ROUNDS = LOADS // RING_SLOTS
PASS_ROUNDS = EXPERT_LOADS // RING_SLOTS
MOD_BATCH = 4
L_MOD = (0, 4, 10, 16, 22, 28)
L_QA, L_KVA, L_QD, L_KD, L_VD, L_QC = (8, 9), 14, (15, 20), (21, 26), (27, 32), 33
L_GL01, L_UQ, L_GL, L_BR, L_OUT, L_SH = 34, 36, 37, 47, 53, 57

Z_JOBS, Z_QC, Z_KVC, Z_GL = 23, 9, 10, 11
PREP_JOBS = 25
NORMS = 7
SQ_PARTS = (4, 1, 1, 1, 4, 4, 4)
UNITS = 18
XR = 2 * KC

VECTOR_STEPS = 255
PASS_STEPS = 98
TAIL_STEPS = 12

ATT = [(br, t, g) for br in "ABC" for t, n in ((0, 2), (1, 4)) for g in range(n)]


def projections_out(job):
    return job + 1 + (job >= 2) + (job >= Z_KVC)


def rope_tables(dim, rows, first):
    half = dim // 4
    inv = (np.float32(ROPE_BASE) ** (-np.arange(half, dtype=np.float32) / np.float32(half))).astype(np.float32)
    tok = np.arange(P)
    pos = np.stack([tok // GRID_W, tok % GRID_W]).astype(np.float32)
    cos, sin, swap = np.ones((P, P), np.float32), np.zeros((P, P), np.float32), np.zeros((P, P), np.float32)
    for r in range(first, rows):
        j = (r - first) % dim
        axis, i = j // (2 * half), j % (2 * half)
        angle = pos[axis] * inv[i % half]
        cos[r], sin[r] = np.cos(angle), np.sin(angle)
        if i < half:
            swap[r + half, r] = -1.0
        else:
            swap[r - half, r] = 1.0
    return cos, sin, swap


CONSTS = ("ident", "ones", "before", "cos_ab", "sin_ab", "swap_ab", "cos_c", "sin_c", "swap_c")


def constants():
    tables = [np.eye(P, dtype=np.float32), np.ones((P, P), np.float32),
              np.triu(np.ones((P, P), np.float32), 1)]
    tables += rope_tables(HD, P, 0)
    tables += rope_tables(C_ROPE, C_QK, C_NOPE)
    tables.append(np.tile(np.arange(SB, dtype=np.float32), (P, 1)))
    lam = [[0.8 - 0.6 * math.exp(-0.3 * l), 1.0 - (0.8 - 0.6 * math.exp(-0.3 * l))] for l in range(DEPTH)]
    return np.concatenate(tables, axis=1), np.array(lam, np.float32)


def hybrid_layers(nc, a, o):
    with ExitStack() as ctx:
        def sb(name, shape, dt=F32):
            return ctx.enter_context(nc.sbuf_tensor(name, shape, dt))

        def sem(name):
            return ctx.enter_context(nc.semaphore(name))

        PS = ctx.enter_context(nc.psum_tensor("PS", [P, 8, 512], F32))

        ring = sb("ring", [P, RING_SLOTS, 2048])
        xT = sb("xT", [P, KC, T])
        const = sb("const", [P, len(CONSTS) * P + SB])
        cst = {n: const[:, i * P:(i + 1) * P] for i, n in enumerate(CONSTS)}
        iota = const[:, len(CONSTS) * P:len(CONSTS) * P + SB]
        ident, ones, before = cst["ident"], cst["ones"], cst["before"]
        condT = sb("condT", [P, KC, 32])
        prow = sb("prow", [84, P])
        parT = sb("parT", [P, 84])
        modT = sb("modT", [P, 48, 2])
        pre1 = sb("pre1", [P, KC, 2])
        post1 = sb("post1", [P, KC, 2])
        pre2 = sb("pre2", [P, KC, 2])
        post2 = sb("post2", [P, KC, 2])
        sink = sb("sink", [P, A_HEADS])
        nsink = sb("nsink", [P, A_HEADS])
        rbias = sb("rbias", [P, N_EXPERTS])
        lamc = sb("lamc", [P, 2])
        lame = sb("lame", [P, 4])
        subl = sb("subl", [P, 1])
        condE = sb("condE", [P, KC, 2])
        negm = sb("negm", [P, 2, 4])
        psums = sb("psums", [P, 2, 4])
        sinke = sb("sinke", [P, 2, 4])
        prec = sb("prec", [P, 2, 4])
        sel = sb("sel", [P, 2, N_EXPERTS])
        gatew = sb("gatew", [P, 2, N_EXPERTS])
        rank = sb("rank", [P, 2, N_EXPERTS])
        count = sb("count", [P, N_EXPERTS])
        npass_i = sb("npass_i", [P, 1], I32)
        off_i = sb("off_i", [P, N_EXPERTS], I32)

        region = sb("region", [P, 23584])

        def view(at, *dims):
            n = math.prod(dims)
            v = region[:, at:at + n]
            if len(dims) == 2:
                return v.rearrange("p (a b) -> p a b", a=dims[0])
            if len(dims) == 3:
                return v.rearrange("p (a b c) -> p a b c", a=dims[0], b=dims[1])
            return v

        gates = view(0, 24, T)
        sq_x = view(0, KC, T)
        w_kvk = view(2048, KC, KV_LORA + C_ROPE)
        st_kb = view(3328, 512)
        st_ka = view(3840, P)
        st_ckv = view(3968, P)
        st_kpe = view(4096, C_QK)
        w_ukv = view(4192, C_HEADS, C_NOPE + C_V)
        qcT = view(5216, 2, T)
        kvcT = view(5728, T)
        hT = view(6144, KC, T)
        qA = view(8192, 4, T)
        qB = view(9216, 4, T)
        qC = view(10240, C_HEADS, T)
        kA = view(12288, 384)
        kB = view(12672, B_HEADS, 384)
        kC = view(14208, C_HEADS, 384)
        vA = view(17280, 3, P)
        vB = view(17664, 3, 512)
        vC = view(19200, 3, 512)
        mod_rows = view(19200, 3, 512)
        sq_lora = view(19200, 3, T)
        prob = view(20736, 2, 512)
        probT = view(21760, 2, 512)
        rope_t = view(20736, 512)
        lam_in = view(21248, 4, HD)
        lam_t = view(21504, 2, HD)
        qcn = view(21760, 2, T)
        ckvT = view(22272, 384)
        state = view(22784, 800)
        sq_od = view(20736, 4, T)
        merged = view(12288, KC, T)
        merge_t = view(22272, 2, T)
        rw = view(21760, KC, N_EXPERTS)
        aT = view(17280, KC, T)
        sq_a = view(6144, KC, T)
        xs = view(0, KC, XSW)
        htok = view(13312, 2, D)
        gsel = view(15360, 2, SB)
        gval = view(16384, 2, SB)
        h2T = view(17408, KC, T)
        gvalT = view(17408, SLOTS // P, T)
        otok = view(15360, 2, D)
        yT = view(20480, KC, T)
        xe = view(15360, 2, KC, CAP)
        hid_rows = view(16384, 2, P)
        hid = view(16640, 2, P)
        sig = view(16896, 2, P)
        act_g = view(17152, P)
        ssig = view(15360, 2, T)
        r_score, r_bias = view(2048, 2, N_EXPERTS), view(2176, 2, N_EXPERTS)
        r_top = view(2304, 2 * N_GROUPS, 8)
        r_gs, r_grep = view(2432, 2, 12), view(2456, 2, 12)
        r_g8, r_gm = view(2480, 2, 8), view(2496, 2, 8)
        r_mask, r_mrep = view(2512, 2, 66), view(2644, 2, 66)
        r_m8, r_sum = view(2776, 2, 8), view(2792, 2)
        r_most, r_np = view(2794, 1), view(2795, 1)

        r_selp, r_val, r_gwp = view(12288, 2, N_EXPERTS), view(12416, 2, N_EXPERTS), view(12544, 2, N_EXPERTS)
        r_cnt, r_junk = view(12672, N_EXPERTS), view(12736, N_EXPERTS)
        r_tmp = view(22528, SB)
        r_scan, r_pos, r_wk = view(23168, 2, 96), view(23360, 2, 8), view(23376, 2, 8)

        def norm_scratch(at, n):
            return [region[:, at + i * n:at + (i + 1) * n] for i in range(3)]

        ring_in = [sem(f"ring_in{i}") for i in range(RING_SLOTS)]
        ring_free = sem("ring_free")
        start_in, consts_in = sem("start_in"), sem("consts_in")
        params_in, weights_in, caches_in, lam_loaded, rw_in = (
            sem("params_in"), sem("weights_in"), sem("caches_in"), sem("lam_loaded"), sem("rw_in"))
        x_ready = sem("x_ready")
        start_tr, cond_exp, cond_ready = sem("start_tr"), sem("cond_exp"), sem("cond_ready")
        params_free, params_tr = sem("params_free"), sem("params_tr")
        mod_done, mod_staged, mod_tr, mod_read, mod_ready = (
            sem("mod_done"), sem("mod_staged"), sem("mod_tr"), sem("mod_read"), sem("mod_ready"))
        sq_ready, ssq_ready, ssq_read, lora_ready = (
            sem("sq_ready"), sem("ssq_ready"), sem("ssq_read"), sem("lora_ready"))
        hn_ready, h_ready = sem("hn_ready"), sem("h_ready")
        z_done, z_ev = sem("z_done"), sem("z_ev")
        gate_ready = sem("gate_ready")
        prep_done, prep_ev = sem("prep_done"), sem("prep_ev")
        sink_exp = sem("sink_exp")
        lam_dot, lam_exp = sem("lam_dot"), sem("lam_exp")
        scores_done, negm_ready, prob_exp, prob_ready, prob_tr, probT_ready, pv_done, o_ready = (
            sem("scores_done"), sem("negm_ready"), sem("prob_exp"), sem("prob_ready"), sem("prob_tr"),
            sem("probT_ready"), sem("pv_done"), sem("o_ready"))
        od_ready = sem("od_ready")
        branch_done, merged_ready = sem("branch_done"), sem("merged_ready")
        wout_done, a_ready, x1_ready = sem("wout_done"), sem("a_ready"), sem("x1_ready")
        router_done, route_exp = sem("router_done"), sem("route_exp")
        htok_tr, htok_ready = sem("htok_tr"), sem("htok_ready")
        shared_gu, shared_exp, shared_hid, shared_down, y_shared = (
            sem("shared_gu"), sem("shared_exp"), sem("shared_hid"), sem("shared_down"), sem("y_shared"))
        sel_ready, rank_done, npass_ready, off_ready = (
            sem("sel_ready"), sem("rank_done"), sem("npass_ready"), sem("off_ready"))
        g_ready, gvt_tr, gvt_ready, gather_done, xs_ready, pad_set = (
            sem("g_ready"), sem("gvt_tr"), sem("gvt_ready"), sem("gather_done"), sem("xs_ready"), sem("pad_set"))
        xe_ready, gu_done, sig_ready, hid_ready, hid_tr, hidT_ready, down_done, out_ready = (
            sem("xe_ready"), sem("gu_done"), sem("sig_ready"), sem("hid_ready"), sem("hid_tr"), sem("hidT_ready"),
            sem("down_done"), sem("out_ready"))
        otok_tr, otok_ready, comb_done, y_ready = (
            sem("otok_tr"), sem("otok_ready"), sem("comb_done"), sem("y_ready"))
        vector_step = sem("vector_step")
        pass_step, expert_step, tail_step, start_step = (
            sem("pass_step"), sem("expert_step"), sem("tail_step"), sem("start_step"))
        state_out, taken = sem("state_out"), sem("taken")
        end_tr, end_ev, y_out = sem("end_tr"), sem("end_ev"), sem("y_out")

        block = ctx.enter_context(nc.Block())

        w_in, w_mod = a["w_in"], a["w_mod"]

        def at_layer(ap, l):
            return ap[ds(l, 1)]

        def cols(ap, l, c0, n):
            return at_layer(ap, l)[:, :, c0:c0 + n].rearrange("o (k p) n -> p (o k) n", p=P)

        def slot_cols(n, width):
            return ring[:, n % RING_SLOTS, 0:KC * width].rearrange("p (k n) -> p k n", k=KC)

        def wide(n):
            return ring[:, n % RING_SLOTS, :].rearrange("p (k n) -> p k n", k=4)

        def down_slot(n):
            return ring[:, n % RING_SLOTS, :].rearrange("p (f n) -> p f n", f=2)

        def apart(engine):
            engine.sem_inc(taken, 1)

        @block.sync
        def _(sp):
            passes = sp.alloc_register("sp_passes")
            sp.reg_mov(passes, 0)
            with sp.Fori(0, DEPTH) as l:
                rounds = sp.snap(l * ROUNDS + sp.snap(passes, min_val=0, max_val=8) * PASS_ROUNDS)

                def load(n, dst, src, base=rounds):
                    sp.wait_ge(ring_free, (base + n // RING_SLOTS) * RING_SLOTS + n % RING_SLOTS + 1)
                    sp.dma_start(dst, src).then_inc(ring_in[n % RING_SLOTS], 16)

                def load_mod(batch):
                    for g in range(MOD_BATCH):
                        n, j = L_MOD[batch] + g, MOD_BATCH * batch + g
                        load(n, slot_cols(n, 256), cols(w_mod, l, 256 * j, 256))

                def load_in(n, c0):
                    load(n, slot_cols(n, 256), cols(w_in, l, c0, 256))

                load_mod(0)
                load_mod(1)
                for j in range(2):
                    w = slot_cols(L_QA[j], 256)
                    for m in range(4):
                        dst, src = w[:, :, m * HD:(m + 1) * HD], cols(w_in, l, QA + 256 * (m % 2) + HD * (2 * j + m // 2), HD)
                        if m == 0:
                            load(L_QA[j], dst, src)
                        else:
                            sp.dma_start(dst, src).then_inc(ring_in[L_QA[j] % RING_SLOTS], 16)
                load_mod(2)
                load_in(L_KVA, KA)
                load_in(L_QD[0], QD)
                load_mod(3)
                load_in(L_QD[1], QD + 256)
                load_in(L_KD[0], KD)
                load_mod(4)
                load_in(L_KD[1], KD + 256)
                load_in(L_VD[0], VD)
                load_mod(5)
                load_in(L_VD[1], VD + 256)
                load(L_QC, slot_cols(L_QC, 256), cols(w_in, l, QC, 256))
                for j in range(2):
                    load(L_GL01 + j, slot_cols(L_GL01 + j, 256), cols(w_in, l, GL + 256 * j, 256))
                load(L_UQ, ring[:, L_UQ % RING_SLOTS, 0:2 * C_HEADS * C_QK].rearrange("p (k n) -> p k n", k=2),
                     at_layer(a["mla_w_uq"], l).rearrange("o (k p) n -> p (o k) n", p=P))
                for j in range(10):
                    load(L_GL + j, slot_cols(L_GL + j, 256), cols(w_in, l, GL + 256 * (j + 2), 256))
                for half in range(2):
                    for b, name in enumerate(("w_branch_a", "w_branch_b", "w_branch_c")):
                        n = L_BR + 3 * half + b
                        load(n, wide(n), at_layer(a[name], l)[:, :, 512 * half:512 * half + 512].rearrange("o (k p) n -> p (o k) n", p=P))
                for j in range(4):
                    load(L_OUT + j, slot_cols(L_OUT + j, 256), cols(a["w_out"], l, 256 * j, 256))
                load(L_SH, slot_cols(L_SH, 256), cols(a["shared_w_gate"], l, 0, 256))
                load(L_SH + 1, slot_cols(L_SH + 1, 256), cols(a["shared_w_up"], l, 0, 256))
                load(L_SH + 2, down_slot(L_SH + 2), at_layer(a["shared_w_down"], l).rearrange("o (f p) n -> p (o f) n", p=P))

                def in_proj(name, e):
                    return at_layer(a[name], l)[:, ds(e, 1)].rearrange("o e (k p) n -> p (o e k) n", p=P)

                def experts_pass(base):
                    def load_gate_up(n, e, base=base):
                        load(n, slot_cols(n, 256), in_proj("moe_w_gate", e), base)
                        load(n + 1, slot_cols(n + 1, 256), in_proj("moe_w_up", e), base)

                    def load_down(n, e, base=base):
                        load(n, down_slot(n), at_layer(a["moe_w_down"], l)[:, ds(e, 1)].rearrange("o e (f p) n -> p (o e f) n", p=P), base)

                    load_gate_up(0, 0)
                    with sp.Fori(0, N_EXPERTS // 4 - 1) as i:
                        for u in range(4):
                            load_gate_up(2 + 3 * u, i * 4 + (u + 1), base + i)
                            load_down(4 + 3 * u, i * 4 + u, base + i)
                    for u in range(4):
                        e = N_EXPERTS - 4 + u
                        if u < 3:
                            load_gate_up(2 + 3 * e, e + 1)
                        load_down(4 + 3 * e - 2 * (u == 3), e)

                experts_pass(rounds + ROUNDS)
                sp.wait_ge(npass_ready, l + 1)
                apart(sp)
                npass = sp.value_load(npass_i[0:1, 0:1], min_val=1, max_val=4)
                with sp.If(npass > 1):
                    with sp.Fori(1, npass) as p:
                        experts_pass(rounds + ROUNDS + p * PASS_ROUNDS)
                    sp.nop()
                sp.reg_add(passes, passes, npass)
                sp.nop()

        @block.gpsimd
        def _(pool):
            stage = view(0, 2, D)
            crow = view(2048, D)
            pool.dma_start(const[:], a["consts"]).then_inc(consts_in, 16)
            pool.dma_start(stage[:, 0, :], a["x_prompt"][0]).then_inc(start_in, 16)
            pool.dma_start(stage[:, 1, :], a["x_sample"][0]).then_inc(start_in, 16)
            pool.dma_start(crow[0:KC, 0:P], a["c_ctx"].rearrange("(k p) -> k p", p=P)).then_inc(start_in, 16)
            pool.dma_start(crow[KC:2 * KC, 0:P], a["c"].rearrange("o (k p) -> (o k) p", p=P)).then_inc(start_in, 16)
            pool.wait_ge(start_tr, 5)
            with pool.Fori(0, DEPTH) as l:
                pool.wait_ge(params_free, l + 1)
                apart(pool)
                r = 0
                for name, n in (("b_mod", 48), ("norm_attn_pre", 8), ("norm_attn_post", 8), ("norm_ffn_pre", 8),
                                ("norm_ffn_post", 8), ("mla_q_norm", 2), ("mla_kv_norm", 1), ("dif_subln", 1)):
                    pool.dma_start(prow[r:r + n, :], at_layer(a[name], l).rearrange("o (k p) -> (o k) p", p=P)).then_inc(params_in, 16)
                    r += n
                pool.dma_start(sink[:], at_layer(a["swa_sink"], l).broadcast_to([P, A_HEADS])).then_inc(params_in, 16)
                pool.dma_start(rbias[:], at_layer(a["router_bias"], l).broadcast_to([P, N_EXPERTS])).then_inc(params_in, 16)
                pool.dma_start(lamc[:], at_layer(a["lam_consts"], l).broadcast_to([P, 2])).then_inc(params_in, 16)
                pool.wait_ge(x_ready, (l + 1) * XR)
                apart(pool)
                for i, name in enumerate(("dif_lq1", "dif_lq2", "dif_lk1", "dif_lk2")):
                    pool.dma_start(lam_in[:, i, :], at_layer(a[name], l).broadcast_to([P, HD])).then_inc(lam_loaded, 16)
                pool.dma_start(st_kb, at_layer(a["cache_dif_k"][0], l).rearrange("o s h m d -> s (o h m d)")).then_inc(caches_in, 16)
                pool.dma_start(st_ka, at_layer(a["cache_swa_k"][0], l).rearrange("o s h d -> s (o h d)")).then_inc(caches_in, 16)
                pool.dma_start(st_ckv, at_layer(a["cache_mla_ckv"][0], l).rearrange("o s d -> s (o d)")).then_inc(caches_in, 16)
                pool.dma_start(st_kpe[:, 0:C_NOPE], at_layer(a["cache_mla_ckv"][0], l)[:, :, 0:C_NOPE].rearrange("o s d -> s (o d)")).then_inc(caches_in, 16)
                pool.dma_start(st_kpe[:, C_NOPE:C_QK], at_layer(a["cache_mla_kpe"][0], l).rearrange("o s d -> s (o d)")).then_inc(caches_in, 16)
                pool.dma_start(vA[:, 2, :], at_layer(a["cache_swa_v"][0], l).rearrange("o s h d -> s (o h d)")).then_inc(caches_in, 16)
                pool.dma_start(vB[:, 2, :], at_layer(a["cache_dif_v"][0], l).rearrange("o s h d -> s (o h d)")).then_inc(caches_in, 16)
                pool.dma_start(w_kvk, cols(w_in, l, KVC, KV_LORA + C_ROPE)).then_inc(weights_in, 16)
                pool.dma_start(w_ukv.rearrange("p h n -> p (h n)"), at_layer(a["mla_w_ukv"], l).rearrange("o p n -> p (o n)")).then_inc(weights_in, 16)
                pool.wait_ge(z_ev, l * projections_out(Z_JOBS - 1) + projections_out(8))
                apart(pool)
                pool.dma_start(at_layer(o["swa_v"][0], l).rearrange("o s h d -> s (o h d)"), vA[:, 0, :]).then_inc(state_out, 16)
                pool.dma_start(at_layer(o["dif_v"][0], l).rearrange("o s h d -> s (o h d)"), vB[:, 0, :]).then_inc(state_out, 16)
                pool.wait_ge(prep_ev, l * PREP_JOBS + 14)
                apart(pool)
                pool.dma_start(at_layer(o["dif_k"][0], l).rearrange("o s h m d -> s (o h m d)"), state[:, 0:512]).then_inc(state_out, 16)
                pool.dma_start(at_layer(o["swa_k"][0], l).rearrange("o s h d -> s (o h d)"), state[:, 512:640]).then_inc(state_out, 16)
                pool.dma_start(at_layer(o["ckv"][0], l).rearrange("o s d -> s (o d)"), state[:, 640:768]).then_inc(state_out, 16)
                pool.dma_start(at_layer(o["kpe"][0], l).rearrange("o s d -> s (o d)"), state[:, 768:800]).then_inc(state_out, 16)
                pool.wait_ge(pv_done, l * UNITS + UNITS)
                apart(pool)
                pool.dma_start(rw, cols(a["router_w"], l, 0, N_EXPERTS)).then_inc(rw_in, 16)
            pool.wait_ge(state_out, DEPTH * 6 * 16)
            fin = view(0, 2, D)
            pool.wait_ge(end_ev, 4)
            pool.dma_start(o["y_prompt"][0], fin[:, 0, :]).then_inc(y_out, 16)
            pool.dma_start(o["y_sample"][0], fin[:, 1, :]).then_inc(y_out, 16)
            pool.wait_ge(y_out, 32)

        @block.tensor
        def _(pe):
            stage = view(0, 2, D)
            crow = view(2048, D)

            def transpose(out, in_, n=P):
                return pe.transpose(out, in_, ident[0:n, 0:n])

            pe.wait_ge(consts_in, 16)
            pe.wait_ge(start_in, 64)
            for j in range(4):
                for c in range(2):
                    for t in range(2):
                        ch = 2 * j + c
                        last = transpose(PS[:, j, (2 * c + t) * P:(2 * c + t + 1) * P], stage[:, t, ch * P:(ch + 1) * P])
                last.then_inc(start_tr, 1)
            transpose(PS[:, 4, 0:2 * KC], crow[0:2 * KC, 0:P], 2 * KC).then_inc(start_tr, 1)
            pe.sem_inc(ring_free, RING_SLOTS)
            pe.wait_ge(cond_ready, 2)

            passes = pe.alloc_register("pe_passes")
            pe.reg_mov(passes, 0)
            with pe.Fori(0, DEPTH) as l:
                before_l = pe.snap(passes, min_val=0, max_val=8)
                rounds = pe.snap(l * ROUNDS + before_l * PASS_ROUNDS)

                def arrived(n, base=None):
                    count = (rounds if base is None else base) + (n // RING_SLOTS + 1)
                    if n % RING_SLOTS in [q % RING_SLOTS for q in L_QA]:
                        count = count + l * 3 + 3 * (base is not None or n >= L_QA[0])
                    pe.wait_ge(ring_in[n % RING_SLOTS], count * 16)

                def sum_squares(n, src, chunks, out, frees=0):
                    before_n = sum(SQ_PARTS[:n])
                    for c in range(chunks):
                        if SQ_PARTS[n] == 4 and c % 2 == 0:
                            pe.wait_ge(sq_ready, l * sum(SQ_PARTS) + (before_n + c // 2 + 1))
                        elif SQ_PARTS[n] == 1 and c == 0:
                            pe.wait_ge(sq_ready, l * sum(SQ_PARTS) + (before_n + 1))
                        last = pe.matmul(out, ones, src[:, c, :], start=(c == 0), stop=(c == chunks - 1))
                        if c == 0 and frees:
                            release(last, frees)
                    return last

                def release(first, loads=1):
                    first.then_inc(ring_free, loads)

                MOD_BANK = (7, 5, 6)

                def mod_batch(batch, frees=0):
                    group, half = divmod(batch, 2)
                    for g in range(MOD_BATCH):
                        arrived(L_MOD[batch] + g)
                    for k in range(KC):
                        for g in range(MOD_BATCH):
                            w = slot_cols(L_MOD[batch] + g, 256)
                            last = pe.matmul(PS[32 * g:32 * g + 32, MOD_BANK[group], half * 256:half * 256 + 256], condT[:, k, :], w[:, k, :],
                                             start=(k == 0), stop=(k == KC - 1), skip_group_check=True)
                            if k == 0 and g == 0 and frees:
                                release(last, frees)
                            if k == KC - 1 and (half == 0 or g < 3):
                                release(last)
                    if half:
                        last.then_inc(mod_done, 1)

                def mod_transposes(group):
                    pe.wait_ge(mod_staged, l * 3 + group + 1)
                    for q_ in range(4):
                        last = transpose(PS[:, MOD_BANK[group], q_ * P:(q_ + 1) * P], mod_rows[:, group, q_ * P:(q_ + 1) * P])
                    last.then_inc(mod_tr, 1)

                mod_batch(0)
                mod_batch(1)
                sum_squares(0, sq_x, KC, PS[:, 0, 0:T], frees=1).then_inc(ssq_ready, 1)
                pe.wait_ge(x_ready, (l + 1) * XR)
                pe.wait_ge(params_in, (l + 1) * 11 * 16)
                transpose(PS[:, 6, 0:84], prow[:], 84).then_inc(params_tr, 1)
                mod_transposes(0)

                def cached_keys():
                    pe.wait_ge(caches_in, (l + 1) * 7 * 16)
                    for h in range(4):
                        last = transpose(PS[:, 2, h * P:(h + 1) * P], st_kb[:, h * P:(h + 1) * P])
                    last.then_inc(prep_done, 1)
                    transpose(PS[:, 3, 0:P], st_ka)
                    transpose(PS[:, 3, P:2 * P], st_ckv)
                    transpose(PS[0:C_QK, 3, 2 * P:3 * P], st_kpe).then_inc(prep_done, 1)

                def bank_emptied(j):
                    if j >= 2:
                        pe.wait_ge(z_ev, l * projections_out(Z_JOBS - 1) + projections_out(j - 2))

                def project(j, n, releases=1):
                    arrived(n)
                    bank_emptied(j)
                    w = slot_cols(n, 256)
                    for m in range(2):
                        for k in range(KC):
                            last = pe.matmul(PS[:, j % 2, m * T:(m + 1) * T], w[:, k, m * P:(m + 1) * P], hT[:, k, :],
                                             start=(k == 0), stop=(k == KC - 1))
                            if m == 0 and k == 0 and releases:
                                release(last)
                    last.then_inc(z_done, 1)

                for j in range(2):
                    arrived(L_QA[j])
                    bank_emptied(j)
                    w = slot_cols(L_QA[j], 256)
                    for m in range(2):
                        for k in range(KC):
                            if j == 0 and m == 0:
                                pe.wait_ge(h_ready, (l * 2 * KC + k + 1) * 2)
                            last = pe.matmul(PS[:, j, m * T:(m + 1) * T], w[:, k, m * P:(m + 1) * P], hT[:, k, :],
                                             start=(k == 0), stop=(k == KC - 1))
                            if j == 1 and m == 0 and k == 0:
                                release(last)
                    last.then_inc(z_done, 1)
                mod_batch(2, frees=1)
                arrived(L_KVA)
                bank_emptied(2)
                w = slot_cols(L_KVA, 256)
                for k in range(KC):
                    last = pe.matmul(PS[:, 0, 0:T], w[:, k, 0:P], hT[:, k, :], start=(k == 0), stop=(k == KC - 1))
                for t in range(2):
                    for k in range(KC):
                        last = pe.matmul(PS[:, 0, T + t * P:T + (t + 1) * P], hT[:, k, t * P:(t + 1) * P], w[:, k, P:2 * P],
                                         start=(k == 0), stop=(k == KC - 1))
                last.then_inc(z_done, 1)
                project(3, L_QD[0])
                mod_batch(3, frees=1)
                cached_keys()
                project(4, L_QD[1])
                project(5, L_KD[0])
                pe.wait_ge(mod_read, l * 3 + 1)
                mod_batch(4, frees=1)
                mod_transposes(1)
                project(6, L_KD[1], 0)

                def project_rows(j, n):
                    arrived(n)
                    bank_emptied(j)
                    w = slot_cols(n, 256)
                    for t in range(2):
                        for k in range(KC):
                            last = pe.matmul(PS[:, j % 2, t * T:(t + 1) * T], hT[:, k, t * P:(t + 1) * P], w[:, k, :],
                                             start=(k == 0), stop=(k == KC - 1))
                            if t == 0 and k == 0:
                                release(last)
                    last.then_inc(z_done, 1)

                project_rows(7, L_VD[0])
                mod_batch(5, frees=1)
                project_rows(8, L_VD[1])
                mod_transposes(2)
                project(Z_QC, L_QC)
                pe.wait_ge(weights_in, (l + 1) * 2 * 16)
                bank_emptied(Z_KVC)
                for k in range(KC):
                    last = pe.matmul(PS[:, 0, 0:T], w_kvk[:, k, 0:P], hT[:, k, :], start=(k == 0), stop=(k == KC - 1))
                    if k == 0:
                        release(last)
                for k in range(KC):
                    last = pe.matmul(PS[0:C_QK, 0, T:2 * T], w_kvk[:, k, C_NOPE:C_NOPE + C_QK], hT[:, k, :],
                                     start=(k == 0), stop=(k == KC - 1))
                last.then_inc(z_done, 1)

                def gate_job(g):
                    project(Z_GL + g, L_GL01 + g if g < 2 else L_GL + g - 2, g > 0)

                def projected(j):
                    pe.wait_ge(z_ev, l * projections_out(Z_JOBS - 1) + projections_out(j))

                def prep_bank(i):
                    if i >= 5:
                        pe.wait_ge(prep_ev, l * PREP_JOBS + i - 4)
                    return 2 + i % 5

                gate_job(0)
                pe.wait_ge(mod_read, l * 3 + 3)
                projected(6)
                for i, src in ((2, qA[:, :, P:T]), (3, qB[:, :, P:T]), (4, kB[:, :, P:T])):
                    b = prep_bank(i)
                    pe.matmul(PS[:, b, :], cst["swap_ab"], src, start=True, stop=True).then_inc(prep_done, 1)
                projected(Z_KVC)
                b = prep_bank(5)
                pe.matmul(PS[:, b, 0:P], cst["swap_ab"], kA[:, P:T], start=True, stop=True)
                pe.matmul(PS[0:C_QK, b, P:T], cst["swap_c"][0:C_QK, 0:C_QK], kC[0:C_QK, 0, P:T], start=True, stop=True).then_inc(prep_done, 1)
                b = prep_bank(6)
                for h in range(4):
                    last = transpose(PS[:, b, h * P:(h + 1) * P], kB[:, h, 0:P])
                last.then_inc(prep_done, 1)
                sum_squares(1, sq_lora, 2, PS[:, 7, 0:T]).then_inc(ssq_ready, 1)
                gate_job(1)
                pe.wait_ge(ssq_read, l * NORMS + 2)
                pe.wait_ge(sq_ready, l * sum(SQ_PARTS) + sum(SQ_PARTS[:3]))
                pe.matmul(PS[:, 7, 0:T], ones, sq_lora[:, 2, :], start=True, stop=True).then_inc(ssq_ready, 1)
                arrived(L_UQ)
                pe.wait_ge(lora_ready, l * 2 + 1)
                w = ring[:, L_UQ % RING_SLOTS, 0:2 * C_HEADS * C_QK].rearrange("p (k n) -> p k n", k=2)
                for i in range(4):
                    b = prep_bank(7 + i)
                    for h in range(2):
                        for k in range(2):
                            last = pe.matmul(PS[0:C_QK, b, h * T:(h + 1) * T], w[:, k, (2 * i + h) * C_QK:(2 * i + h + 1) * C_QK],
                                             qcn[:, k, :], start=(k == 0), stop=(k == 1))
                            if i == 0 and h == 0 and k == 0:
                                release(last)
                    last.then_inc(prep_done, 1)
                project(Z_GL + 2, L_GL)
                for i in range(2):
                    b = prep_bank(11 + i)
                    pe.wait_ge(prep_ev, l * PREP_JOBS + 9 + 2 * i)
                    pe.matmul(PS[0:C_QK, b, :], cst["swap_c"][0:C_QK, 0:C_QK], qC[0:C_QK, 4 * i:4 * i + 4, P:T],
                              start=True, stop=True).then_inc(prep_done, 1)
                pe.wait_ge(lora_ready, l * 2 + 2)
                b = prep_bank(13)
                transpose(PS[:, b, 0:P], kA[:, 0:P])
                transpose(PS[:, b, P:2 * P], ckvT[:, 0:P])
                transpose(PS[:, b, 2 * P:2 * P + C_QK], kC[0:C_QK, 0, 0:P], C_QK).then_inc(prep_done, 1)
                gate_job(3)
                for h in range(C_HEADS):
                    b = prep_bank(14 + h)
                    pe.matmul(PS[0:C_NOPE, b, 0:384], w_ukv[:, h, 0:C_NOPE], ckvT, start=True, stop=True).then_inc(prep_done, 1)
                for t in range(3):
                    b = prep_bank(22 + t)
                    pe.matmul(PS[:, b, :], ckvT[:, t * P:(t + 1) * P], w_ukv[:, :, C_NOPE:C_NOPE + C_V],
                              start=True, stop=True).then_inc(prep_done, 1)

                def scores(u):
                    br, t, g = ATT[u]
                    b = 2 + 2 * (u % 2)
                    q0, k0, kn = t * P, t * P, P + t * P
                    if u < 2:
                        pe.wait_ge(prep_ev, l * PREP_JOBS + PREP_JOBS)
                    else:
                        pe.wait_ge(prob_exp, (l * UNITS + u - 1) * 4)
                    n = 4 if t == 0 else 2
                    for i in range(n):
                        if br == "A":
                            h = n * g + i
                            kv, c = h // 4, h % 4
                            last = pe.matmul(PS[:, b, i * kn:(i + 1) * kn], qA[HD * kv:HD * (kv + 1), c, q0:q0 + P],
                                             kA[HD * kv:HD * (kv + 1), k0:k0 + kn], start=True, stop=True)
                        elif br == "B":
                            j, m = divmod(i, 2)
                            h = (n // 2) * g + j
                            last = pe.matmul(PS[:, b + m, j * kn:(j + 1) * kn], qB[HD * m:HD * (m + 1), h, q0:q0 + P],
                                             kB[HD * m:HD * (m + 1), h, k0:k0 + kn], start=True, stop=True)
                        else:
                            h = n * g + i
                            last = pe.matmul(PS[:, b, i * kn:(i + 1) * kn], qC[0:C_QK, h, q0:q0 + P],
                                             kC[0:C_QK, h, k0:k0 + kn], start=True, stop=True)
                    last.then_inc(scores_done, 1)

                def transposes(u):
                    br = ATT[u][0]
                    pe.wait_ge(prob_ready, l * UNITS + u + 1)
                    if u >= 1:
                        pe.wait_ge(probT_ready, l * UNITS + u)
                    for i in range(2 if br == "B" else 4):
                        last = transpose(PS[:, 6, i * P:(i + 1) * P], prob[:, u % 2, i * P:(i + 1) * P])
                    last.then_inc(prob_tr, 1)

                def weighted_values(u):
                    br, t, g = ATT[u]
                    pe.wait_ge(probT_ready, l * UNITS + u + 1)
                    if u >= 1:
                        pe.wait_ge(o_ready, l * UNITS + u)
                    heads = (2 if t == 0 else 1) if br == "B" else (4 if t == 0 else 2)
                    for kt in range(t + 1):
                        for i in range(heads):
                            h = heads * g + i
                            tile = kt + t
                            if br == "A":
                                v = vA[:, tile, (h // 4) * HD:(h // 4 + 1) * HD]
                            elif br == "B":
                                v = vB[:, tile, h * P:(h + 1) * P]
                            else:
                                v = vC[:, tile, h * C_V:(h + 1) * C_V]
                            if br == "B":
                                out = PS[:, 7, i * P:(i + 1) * P]
                            else:
                                out = PS[HD * (i % 2):HD * (i % 2) + HD, 7, (i // 2) * P:(i // 2 + 1) * P]
                            blk = i * (t + 1) + kt
                            last = pe.matmul(out, v, probT[:, u % 2, blk * P:(blk + 1) * P], start=(kt == 0), stop=(kt == t),
                                             skip_group_check=True)
                    last.then_inc(pv_done, 1)

                for s in range(UNITS + 2):
                    if s < UNITS:
                        scores(s)
                    if s % 2 == 0 and s // 2 + 4 < 12:
                        gate_job(s // 2 + 4)
                    if 1 <= s <= UNITS:
                        transposes(s - 1)
                    if s >= 2:
                        weighted_values(s - 2)

                pe.wait_ge(sq_ready, l * sum(SQ_PARTS) + sum(SQ_PARTS[:4]))
                for i in range(2):
                    last = pe.matmul(PS[:, 4 + i, :], ones, sq_od[:, 2 * i:2 * i + 2, :], start=True, stop=True)
                last.then_inc(ssq_ready, 1)

                pe.wait_ge(gate_ready, (l + 1) * 12)
                order = [(0, 0), (0, 1), (1, 0), (1, 1), (0, 2), (1, 2)] + [(j, n) for j in range(2, KC) for n in range(3)]
                for j, n in order:
                    half, jj = divmod(j, 4)
                    b = 2 * (j % 2)
                    src, br = ((qA, 0), (qC, 2), (qB, 1))[n]
                    if n == 0 and j >= 2:
                        pe.wait_ge(merged_ready, l * KC + j - 1)
                    if jj == 0:
                        arrived(L_BR + 3 * half + br)
                    if n == 0 and j == 0:
                        pe.wait_ge(o_ready, l * UNITS + UNITS)
                    if n == 2 and j == 0:
                        pe.wait_ge(od_ready, l + 1)
                    w = wide(L_BR + 3 * half + br)
                    for k in range(4):
                        last = pe.matmul(PS[:, b + n // 2, (n % 2) * T:(n % 2 + 1) * T], w[:, k, jj * P:(jj + 1) * P], src[:, k, :],
                                         start=(k == 0), stop=(k == 3))
                        if n == 0 and k == 0 and jj == 0:
                            release(last, 1 if half == 0 else 3)
                    if n == 2:
                        last.then_inc(branch_done, 1)
                for j in range(4):
                    arrived(L_OUT + j)
                    w = slot_cols(L_OUT + j, 256)
                    for m in range(2):
                        for k in range(KC):
                            if j == 0 and m == 0:
                                pe.wait_ge(merged_ready, l * KC + k + 1)
                            last = pe.matmul(PS[:, 4 + j, m * T:(m + 1) * T], w[:, k, m * P:(m + 1) * P], merged[:, k, :],
                                             start=(k == 0), stop=(k == KC - 1))
                            if m == 0 and k == 0:
                                release(last, 3 if j == 0 else 1)
                    last.then_inc(wout_done, 1)
                sum_squares(4, sq_a, KC, PS[:, 0, 0:T]).then_inc(ssq_ready, 1)
                sum_squares(5, sq_x, KC, PS[:, 1, 0:T]).then_inc(ssq_ready, 1)

                pe.wait_ge(rw_in, (l + 1) * 16)
                pe.wait_ge(h_ready, (l * 2 * KC + 2 * KC) * 2)
                for t in range(2):
                    for k in range(KC):
                        last = pe.matmul(PS[:, 0, t * N_EXPERTS:(t + 1) * N_EXPERTS], h2T[:, k, t * P:(t + 1) * P], rw[:, k, :],
                                         start=(k == 0), stop=(k == KC - 1))
                        if t == 0 and k == 0:
                            release(last)
                last.then_inc(router_done, 1)
                arrived(L_SH)
                arrived(L_SH + 1)
                for n in range(2):
                    w = slot_cols(L_SH + n, 256)
                    for m in range(2):
                        for k in range(KC):
                            last = pe.matmul(PS[:, 6 + n, m * T:(m + 1) * T], w[:, k, m * P:(m + 1) * P], h2T[:, k, :],
                                             start=(k == 0), stop=(k == KC - 1))
                    if n == 0:
                        pe.wait_ge(sel_ready, l + 1)
                        pe.matmul(PS[:, 1, 0:64], before, sel[:, 0, :], start=True, stop=True)
                        pe.matmul(PS[:, 1, 64:128], before, sel[:, 1, :], start=True, stop=False)
                        pe.matmul(PS[:, 1, 64:128], ones, sel[:, 0, :], start=False, stop=True)
                        pe.matmul(PS[:, 1, 128:192], ones, sel[:, 0, :], start=True, stop=False)
                        pe.matmul(PS[:, 1, 128:192], ones, sel[:, 1, :], start=False, stop=True).then_inc(rank_done, 1)
                last.then_inc(shared_gu, 1)
                for j in range(4):
                    t, half = divmod(j, 2)
                    for c in range(4):
                        ch = 4 * half + c
                        last = transpose(PS[:, 2 + j, c * P:(c + 1) * P], h2T[:, ch, t * P:(t + 1) * P])
                        if j == 0 and c == 0:
                            release(last, 2)
                    last.then_inc(htok_tr, 1)
                arrived(L_SH + 2)
                pe.wait_ge(shared_hid, l + 1)
                shid = view(0, 2, T)
                w = down_slot(L_SH + 2)
                for j in range(4):
                    pe.wait_ge(htok_ready, l * 4 + j + 1)
                    for c in range(2):
                        for f in range(2):
                            last = pe.matmul(PS[:, 2 + j, c * T:(c + 1) * T], w[:, f, (2 * j + c) * P:(2 * j + c + 1) * P], shid[:, f, :],
                                             start=(f == 0), stop=(f == 1))
                    last.then_inc(shared_down, 1)
                pe.wait_ge(shared_down, (l + 1) * 4)
                pe.sem_inc(ring_free, 1)
                pe.wait_ge(npass_ready, l + 1)
                apart(pe)
                npass = pe.value_load(npass_i[0:1, 0:1], min_val=1, max_val=4)

                with pe.Fori(0, npass) as p:
                    q = pe.snap(before_l + p)
                    base = pe.snap(rounds + ROUNDS + p * PASS_ROUNDS)
                    for blk in range(NSB):
                        pe.wait_ge(g_ready, q * NSB + blk + 1)
                        for pair in range(2):
                            n = 2 * blk + pair
                            if n >= 2:
                                pe.wait_ge(gvt_ready, q * 2 * NSB + n - 1)
                            for i in range(2):
                                for t in range(2):
                                    c0 = (2 * pair + i) * P
                                    last = transpose(PS[:, 6 + n % 2, (2 * i + t) * P:(2 * i + t + 1) * P], gval[:, t, c0:c0 + P])
                            last.then_inc(gvt_tr, 1)
                        for c in range(KC):
                            n = KC * blk + c
                            if n == 0:
                                pe.wait_ge(y_shared, l * 4 + 4)
                            if n >= 4:
                                pe.wait_ge(xs_ready, q * NSB * KC + n - 3)
                            for t in range(2):
                                last = pe.matmul(PS[:, 2 + n % 4, :], htok[:, t, c * P:(c + 1) * P], gsel[:, t, :],
                                                 start=(t == 0), stop=(t == 1))
                            last.then_inc(gather_done, 1)
                    pe.wait_ge(off_ready, q + 1)
                    pe.wait_ge(pad_set, l + 1)

                    def gate_or_up(n, half, odd, base, frees=1):
                        arrived(n + half, base)
                        w = slot_cols(n + half, 256)
                        for k in range(KC):
                            for f in range(2):
                                last = pe.matmul(PS[f * CAP:(f + 1) * CAP, odd, half * P:(half + 1) * P], xe[:, odd, k, :],
                                                 w[:, k, f * P:(f + 1) * P], start=(k == 0), stop=(k == KC - 1), skip_group_check=True)
                                if k == 0 and f == 0 and frees:
                                    release(last, frees)
                        if half:
                            last.then_inc(gu_done, 1)

                    def transpose_hidden(e, odd):
                        pe.wait_ge(hid_ready, q * N_EXPERTS + e + 1)
                        transpose(PS[:, 6 + odd, 0:P], hid_rows[:, odd, :]).then_inc(hid_tr, 1)

                    def down(n, e, odd, base, waits=True):
                        arrived(n, base)
                        pe.wait_ge(hidT_ready, q * N_EXPERTS + e + 1)
                        if waits:
                            pe.wait_ge(out_ready, q * N_EXPERTS + e - 1)
                        w = down_slot(n)
                        for c in range(KC):
                            for f in range(2):
                                last = pe.matmul(PS[:, 2 + odd, c * CAP:(c + 1) * CAP], w[:, f, c * P:(c + 1) * P],
                                                 hid[:, odd, f * CAP:(f + 1) * CAP], start=(f == 0), stop=(f == 1))
                                if c == 0 and f == 0:
                                    release(last)
                        last.then_inc(down_done, 1)

                    def expert(u, e, base, waits=True):
                        odd, nxt = u % 2, (u + 1) % 2
                        pe.wait_ge(xe_ready, q * N_EXPERTS + e + 2)
                        gate_or_up(2 + 3 * u, 0, nxt, base)
                        transpose_hidden(e, odd)
                        gate_or_up(2 + 3 * u, 1, nxt, base)
                        down(4 + 3 * u, e, odd, base, waits)

                    pe.wait_ge(xe_ready, q * N_EXPERTS + 1)
                    gate_or_up(0, 0, 0, base, frees=0)
                    gate_or_up(0, 1, 0, base)
                    for e in range(2):
                        expert(e, e, base, waits=False)
                    with pe.Fori(0, N_EXPERTS // 4 - 1) as i:
                        for u in range(2, 6):
                            expert(u, i * 4 + u, base + i)
                    expert(N_EXPERTS - 2, N_EXPERTS - 2, base)
                    e = N_EXPERTS - 1
                    transpose_hidden(e, e % 2)
                    down(2 + 3 * e, e, e % 2, base)
                    pe.wait_ge(out_ready, (q + 1) * N_EXPERTS)
                    pe.wait_ge(gvt_ready, (q + 1) * 2 * NSB)
                    for s in range(SLOTS // P + 1):
                        if s < SLOTS // P:
                            if s >= 1:
                                pe.wait_ge(otok_ready, q * 12 + s)
                            for c in range(KC):
                                last = transpose(PS[:, 4 + c // 4, (c % 4) * P:(c % 4 + 1) * P], xs[:, c, s * P:(s + 1) * P])
                                if s == 0 and c == 0:
                                    release(last)
                            last.then_inc(otok_tr, 1)
                        if s >= 1:
                            r = s - 1
                            pe.wait_ge(otok_ready, q * 12 + r + 1)
                            for c in range(KC):
                                last = pe.matmul(PS[:, c // 2, (c % 2) * T:(c % 2 + 1) * T], otok[:, r % 2, c * P:(c + 1) * P], gvalT[:, r, :],
                                                 start=(r == 0 and c % 2 == 0), stop=(r == SLOTS // P - 1), skip_group_check=True)
                            last.then_inc(comb_done, 1)
                    pe.wait_ge(y_ready, (q + 1) * 4)
                pe.reg_add(passes, passes, npass)
                sum_squares(6, view(0, KC, T), KC, PS[:, 4, 0:T]).then_inc(ssq_ready, 1)
            pe.wait_ge(x_ready, (DEPTH + 1) * XR)
            for j in range(4):
                t, half = divmod(j, 2)
                for c in range(4):
                    last = transpose(PS[:, j, c * P:(c + 1) * P], xT[:, 4 * half + c, t * P:(t + 1) * P])
                last.then_inc(end_tr, 1)

        @block.scalar
        def _(act):
            def bank(b):
                return PS[:, b, :]

            def halves(b):
                return b.rearrange("p (m t) -> p m t", m=2)

            act.wait_ge(start_tr, 5)
            act.activation(condE[:], PS[:, 4, 0:2 * KC].rearrange("p (t k) -> p k t", t=2), ACT.Exp, scale=-1.0).then_inc(cond_exp, 1)
            passes = act.alloc_register("act_passes")
            act.reg_mov(passes, 0)
            with act.Fori(0, DEPTH) as l:
                before_l = act.snap(passes, min_val=0, max_val=8)

                def squares(dst, src):
                    act.activation(dst, src, ACT.Square).then_inc(sq_ready, 1)

                def squares_in_parts(dst, src, part_ready):
                    for part in range(4):
                        part_ready(part)
                        squares(dst[:, 2 * part:2 * part + 2, :], src[:, 2 * part:2 * part + 2, :])

                def modulate(call, dst, scale, shift):
                    act.wait_ge(mod_ready, l * 2 + call + 1)
                    for c in range(KC):
                        act.wait_ge(hn_ready, l * 2 * KC + call * KC + c + 1)
                        for t in range(2):
                            act.activation(dst[:, c, t * P:(t + 1) * P], dst[:, c, t * P:(t + 1) * P], ACT.Identity,
                                           scale=scale[:, c, t:t + 1], bias=shift[:, c, t:t + 1]).then_inc(h_ready, 1)

                def projected(j):
                    act.wait_ge(z_done, l * Z_JOBS + j + 1)
                    return bank(j % 2)

                squares_in_parts(sq_x, xT, lambda part: act.wait_ge(x_ready, l * XR + 4 * (part + 1)))
                act.wait_ge(x_ready, (l + 1) * XR)

                def stage_mod(group):
                    act.wait_ge(mod_done, l * 3 + group + 1)
                    act.activation(mod_rows[:, group, :], bank((7, 5, 6)[group]), ACT.Copy).then_inc(mod_staged, 1)

                stage_mod(0)
                modulate(0, hT, pre1, modT[:, 0:KC, :])

                for j in range(2):
                    act.activation(qA[:, 2 * j:2 * j + 2, :], halves(projected(j)), ACT.Copy).then_inc(z_ev, 1)
                b = projected(2)
                act.activation(kA[:, 0:T], b[:, 0:T], ACT.Copy).then_inc(z_ev, 1)
                act.activation(vA[:, 0:2, :], halves(b[:, T:2 * T]), ACT.Copy).then_inc(z_ev, 1)
                for j in (3, 4):
                    if j == 4:
                        stage_mod(1)
                    act.activation(qB[:, 2 * j - 6:2 * j - 4, :], halves(projected(j)), ACT.Copy).then_inc(z_ev, 1)
                for j in (5, 6):
                    act.activation(kB[:, 2 * j - 10:2 * j - 8, 0:T], halves(projected(j)), ACT.Copy).then_inc(z_ev, 1)
                for j in (7, 8):
                    if j == 8:
                        stage_mod(2)
                    act.activation(vB[:, 0:2, (j - 7) * T:(j - 6) * T], halves(projected(j)), ACT.Copy).then_inc(z_ev, 1)
                act.activation(qcT, halves(projected(Z_QC)), ACT.Copy).then_inc(z_ev, 1)
                b = projected(Z_KVC)
                act.activation(kvcT, b[:, 0:T], ACT.Copy).then_inc(z_ev, 1)
                act.activation(kC[0:C_QK, 0, 0:T], b[0:C_QK, T:2 * T], ACT.Copy).then_inc(z_ev, 1)
                act.wait_ge(z_ev, l * projections_out(Z_JOBS - 1) + projections_out(Z_KVC))
                act.wait_ge(mod_tr, l * 3 + 3)
                squares(sq_lora[:, 0:2, :], qcT)
                squares(sq_lora[:, 2, :], kvcT)
                act.wait_ge(lam_dot, l + 1)
                act.activation(lame[:, 0:2], lame[:, 2:4], ACT.Exp).then_inc(lam_exp, 1)

                def gate_exp(g):
                    act.activation(gates[:, 2 * g:2 * g + 2, :], halves(projected(Z_GL + g)), ACT.Exp, scale=-1.0).then_inc(z_ev, 1)

                for g in range(4):
                    gate_exp(g)

                def exponentiate(u):
                    br, t, g = ATT[u]
                    act.wait_ge(negm_ready, l * UNITS + u + 1)
                    b = 2 + 2 * (u % 2)
                    n, kn = (4, P) if t == 0 else (2, 2 * P)
                    if u >= 2:
                        act.wait_ge(prob_tr, l * UNITS + u - 1)
                    if br == "A":
                        act.activation(sinke[:, u % 2, 0:n], sinke[:, u % 2, 0:n], ACT.Exp).then_inc(sink_exp, 1)
                    for i in range(n):
                        m, j = divmod(i, n // 2)
                        src = PS[:, b + m, j * kn:(j + 1) * kn] if br == "B" else PS[:, b, i * kn:(i + 1) * kn]
                        act.activation(prob[:, u % 2, i * kn:(i + 1) * kn], src, ACT.Exp,
                                       scale=(C_QK if br == "C" else HD) ** -0.5, bias=negm[:, u % 2, i:i + 1],
                                       accum_out=psums[:, u % 2, i:i + 1]).then_inc(prob_exp, 4 // n)

                def copy_probT(u):
                    n = 2 if ATT[u][0] == "B" else 4
                    act.wait_ge(prob_tr, l * UNITS + u + 1)
                    if u >= 2:
                        act.wait_ge(pv_done, l * UNITS + u - 1)
                    act.activation(probT[:, u % 2, 0:n * P], PS[:, 6, 0:n * P], ACT.Copy).then_inc(probT_ready, 1)

                act.wait_ge(prep_ev, l * PREP_JOBS + PREP_JOBS)
                for s in range(UNITS + 1):
                    if s < UNITS:
                        exponentiate(s)
                    if s % 2 == 0 and s // 2 + 4 < 12:
                        gate_exp(s // 2 + 4)
                    if s >= 1:
                        copy_probT(s - 1)
                act.wait_ge(o_ready, l * UNITS + 12)
                squares(sq_od, qB)

                act.wait_ge(state_out, (l + 1) * 6 * 16)
                for j in range(4):
                    act.wait_ge(wout_done, l * 4 + j + 1)
                    act.activation(aT[:, 2 * j:2 * j + 2, :], halves(bank(4 + j)), ACT.Copy).then_inc(a_ready, 1)
                    act.wait_ge(a_ready, l * 4 + j + 1)
                    squares(sq_a[:, 2 * j:2 * j + 2, :], aT[:, 2 * j:2 * j + 2, :])
                squares_in_parts(sq_x, xT, lambda part: act.wait_ge(x1_ready, l * 2 * KC + 4 * (part + 1)))
                modulate(1, h2T, pre2, modT[:, 24:32, :])

                act.wait_ge(router_done, l + 1)
                act.activation(r_score, bank(0)[:, 0:2 * N_EXPERTS].rearrange("p (t e) -> p t e", t=2), ACT.Exp, scale=-1.0).then_inc(route_exp, 1)
                act.wait_ge(shared_gu, l + 1)
                act.activation(ssig, halves(bank(6)), ACT.Exp, scale=-1.0).then_inc(shared_exp, 1)
                for j in range(4):
                    t, half = divmod(j, 2)
                    act.wait_ge(htok_tr, l * 4 + j + 1)
                    act.activation(htok[:, t, half * 512:(half + 1) * 512], bank(2 + j), ACT.Copy).then_inc(htok_ready, 1)
                for j in range(4):
                    act.wait_ge(shared_down, l * 4 + j + 1)
                    act.activation(yT[:, 2 * j:2 * j + 2, :], halves(bank(2 + j)), ACT.Copy).then_inc(y_shared, 1)
                act.wait_ge(npass_ready, l + 1)
                apart(act)
                npass = act.value_load(npass_i[0:1, 0:1], min_val=1, max_val=4)
                with act.Fori(0, npass) as p:
                    q = act.snap(before_l + p)
                    for blk in range(NSB):
                        for pair in range(2):
                            n = 2 * blk + pair
                            act.wait_ge(gvt_tr, q * 2 * NSB + n + 1)
                            act.activation(gvalT[:, 4 * blk + 2 * pair:4 * blk + 2 * pair + 2, :], halves(bank(6 + n % 2)), ACT.Copy).then_inc(gvt_ready, 1)
                        for c in range(KC):
                            n = KC * blk + c
                            act.wait_ge(gather_done, q * NSB * KC + n + 1)
                            act.activation(xs[:, c, CAP + blk * SB:CAP + (blk + 1) * SB], bank(2 + n % 4), ACT.Copy).then_inc(xs_ready, 1)
                    act.wait_ge(off_ready, q + 1)
                    act.wait_ge(xs_ready, (q + 1) * NSB * KC)

                    act.wait_ge(gvt_ready, (q + 1) * 2 * NSB)
                    apart(act)

                    def offset(e):
                        return act.value_load(off_i[0:1, ds(e, 1)], min_val=0, max_val=SLOTS)

                    def take_inputs(e, odd, waits=True):
                        off = offset(e)
                        if waits:
                            act.wait_ge(gu_done, q * N_EXPERTS + e - 1)
                        act.activation(xe[:, odd], xs[:, :, ds(off + CAP, CAP)], ACT.Copy).then_inc(xe_ready, 1)

                    def sigmoid_exp(e, odd, waits=True):
                        act.wait_ge(gu_done, q * N_EXPERTS + e + 1)
                        if waits:
                            act.wait_ge(hid_ready, q * N_EXPERTS + e - 1)
                        act.activation(sig[:, odd, :], PS[:, odd, 0:P], ACT.Exp, scale=-1.0).then_inc(sig_ready, 1)

                    def put_out(e, odd, waits=True):
                        off = offset(e)
                        act.wait_ge(down_done, q * N_EXPERTS + e + 1)
                        act.wait_ge(xe_ready, q * N_EXPERTS + e + 1)
                        if waits:
                            act.wait_ge(out_ready, q * N_EXPERTS + e)
                        act.activation(xs[:, :, ds(off, CAP)], PS[:, 2 + odd, :].rearrange("p (c s) -> p c s", c=KC), ACT.Copy).then_inc(out_ready, 1)

                    take_inputs(0, 0, waits=False)
                    take_inputs(1, 1, waits=False)
                    sigmoid_exp(0, 0, waits=False)
                    take_inputs(2, 0)
                    sigmoid_exp(1, 1, waits=False)
                    take_inputs(3, 1)
                    put_out(0, 0, waits=False)
                    with act.Fori(0, N_EXPERTS // 2 - 2) as i:
                        for u in range(2):
                            e = i * 2 + (1 + u)
                            sigmoid_exp(e + 1, u)
                            take_inputs(e + 3, u)
                            put_out(e, 1 - u)
                    for e in range(N_EXPERTS - 3, N_EXPERTS):
                        if e < N_EXPERTS - 1:
                            sigmoid_exp(e + 1, (e + 1) % 2)
                        put_out(e, e % 2)
                    for s in range(SLOTS // P):
                        act.wait_ge(otok_tr, q * 12 + s + 1)
                        if s >= 2:
                            act.wait_ge(comb_done, q * 12 + s - 1)
                        act.activation(otok[:, s % 2, :], PS[:, 4:6, :].rearrange("p a b -> p (a b)"), ACT.Copy).then_inc(otok_ready, 1)
                squares_in_parts(view(0, KC, T), yT, lambda part: part or act.wait_ge(y_ready, (before_l + npass) * 4))
                act.reg_add(passes, passes, npass)
            for j in range(4):
                t, half = divmod(j, 2)
                act.wait_ge(end_tr, j + 1)
                act.activation(view(0, 2, D)[:, t, half * 512:(half + 1) * 512], bank(j), ACT.Copy).then_inc(end_ev, 1)

        @block.vector
        def _(dve):
            ve = nc.vector

            class Chain:

                def __init__(self, semaphore, base):
                    self.semaphore, self.base, self.n = semaphore, base, 0

                def __call__(self, ins, own=False):
                    self.add(ins)
                    dve.wait_ge(self.semaphore, self.base + self.n)
                    if own:
                        apart(dve)

                def add(self, ins):
                    self.n += 1
                    ins.then_inc(self.semaphore, 1)

            start = Chain(start_step, 0)
            for j in range(4):
                dve.wait_ge(start_tr, j + 1)
                ve.tensor_copy(xT[:, 2 * j:2 * j + 2, :], PS[:, j, :].rearrange("p (c t) -> p c t", c=2)).then_inc(x_ready, XR // 4)
            dve.wait_ge(cond_exp, 1)
            start(ve.tensor_scalar(condE[:], condE[:], 1.0, None, ALU.add))
            start(ve.reciprocal(condE[:], condE[:]))
            dve.wait_ge(start_tr, 5)
            ve.memset(condT[:, :, 2:32], 0.0).then_inc(cond_ready, 1)
            ve.tensor_tensor(condT[:, :, 0:2], PS[:, 4, 0:2 * KC].rearrange("p (t k) -> p k t", t=2), condE[:], ALU.mult).then_inc(cond_ready, 1)

            dve.sem_inc(params_free, 1)
            passes = dve.alloc_register("dve_passes")
            dve.reg_mov(passes, 0)
            with dve.Fori(0, DEPTH) as l:
                before_l = dve.snap(passes, min_val=0, max_val=8)
                step = Chain(vector_step, l * VECTOR_STEPS)

                def per_column(v, shape, axis):
                    return v.unsqueeze(axis).broadcast_to(shape)

                def rstd(n, src, channels, scratch):
                    var, y, t = scratch
                    dve.wait_ge(ssq_ready, l * NORMS + n + 1)
                    ve.tensor_scalar(var, src, 1.0 / channels, EPS, ALU.mult, ALU.add).then_inc(ssq_read, 1)
                    dve.wait_ge(ssq_read, l * NORMS + n + 1)
                    step(ve.tensor_scalar(t.bitcast(I32), var.bitcast(I32), 1, None, ALU.arith_shift_right))
                    step(ve.tensor_scalar(y.bitcast(I32), t.bitcast(I32), -1.0, float(0x5F3759DF), ALU.mult, ALU.add))
                    for _ in range(3):
                        step(ve.scalar_tensor_tensor(out=t, in0=y, scalar=-0.5, in1=y, op0=ALU.mult, op1=ALU.mult))
                        step(ve.tensor_tensor(t, t, var, ALU.mult))
                        step(ve.scalar_tensor_tensor(out=y, in0=t, scalar=1.5, in1=y, op0=ALU.add, op1=ALU.mult))
                    return y

                def normalise_x(n, dst, src, scratch):
                    r = rstd(n, src, D, scratch)
                    for c in range(KC):
                        ve.tensor_tensor(dst[:, c, :], xT[:, c, :], r, ALU.mult).then_inc(hn_ready, 1)

                def add_normalised(n, a_, src, post, scratch, done):
                    r = rstd(n, src, D, scratch)
                    step(ve.tensor_tensor(a_, a_, per_column(r, [P, KC, T], 1), ALU.mult))
                    for c in range(KC):
                        for t in range(2):
                            xs_ = xT[:, c, t * P:(t + 1) * P]
                            ve.scalar_tensor_tensor(out=xs_, in0=a_[:, c, t * P:(t + 1) * P], scalar=post[:, c, t:t + 1], in1=xs_,
                                                    op0=ALU.mult, op1=ALU.add).then_inc(done, 1)

                dve.wait_ge(x_ready, (l + 1) * XR)
                normalise_x(0, hT, PS[:, 0, 0:T], norm_scratch(21760, T))
                dve.wait_ge(params_tr, l + 1)
                step(ve.tensor_copy(parT[:], PS[:, 6, 0:84]))
                dve.wait_ge(params_in, (l + 1) * 11 * 16)
                step(ve.tensor_scalar(nsink[:], sink[:], -1.0, None, ALU.mult))
                step(ve.tensor_scalar(subl[:], parT[:, 83:84], lamc[:, 1:2], None, ALU.mult))

                def gain(c0, n=KC):
                    return per_column(parT[:, c0:c0 + n], [P, n, 2], 2)

                def mod_add(group):
                    dve.wait_ge(mod_tr, l * 3 + group + 1)
                    src = PS[:, (7, 5, 6)[group], :].rearrange("p (a b g r) -> p a g b r", a=2, b=2, g=4)
                    for a_ in range(2):
                        m = 16 * group + 8 * a_
                        dst = modT[:, m:m + 8, :].rearrange("p (g b) t -> p g b t", b=2)
                        bias = parT[:, m:m + 8].rearrange("p (g b) -> p g b", b=2).unsqueeze(3).broadcast_to([P, 4, 2, 2])
                        ins = ve.tensor_tensor(dst, src[:, a_, :, :, 0:2], bias, ALU.add)
                        if a_ == 0:
                            step(ins)
                        else:
                            ins.then_inc(mod_read, 1)
                    dve.wait_ge(mod_read, l * 3 + group + 1)

                mod_add(0)
                ve.scalar_tensor_tensor(out=pre1[:], in0=modT[:, 8:16, :], scalar=1.0, in1=gain(48), op0=ALU.add, op1=ALU.mult).then_inc(mod_ready, 1)

                def prep(i):
                    dve.wait_ge(prep_done, l * PREP_JOBS + i + 1)
                    return PS[:, 2 + i % 5, :]

                b = prep(0)
                ve.tensor_copy(kB[:, :, T:T + P], b.rearrange("p (h s) -> p h s", h=4)).then_inc(prep_ev, 1)
                b = prep(1)
                step(ve.tensor_copy(kA[:, T:T + P], b[:, 0:P]))
                step(ve.tensor_copy(ckvT[:, T:T + P], b[:, P:2 * P]))
                ve.tensor_copy(kC[C_NOPE:C_QK, :, T:T + P], per_column(b[C_NOPE:C_QK, 2 * P:3 * P], [C_ROPE, C_HEADS, P], 1)).then_inc(prep_ev, 1)
                dve.wait_ge(lam_loaded, (l + 1) * 4 * 16)
                step(ve.tensor_tensor(lam_t, lam_in[:, 0:2, :], lam_in[:, 2:4, :], ALU.mult))
                ve.reduce_sum(lame[:, 2:4], lam_t, X).then_inc(lam_dot, 1)
                mod_add(1)
                mod_add(2)
                step(ve.scalar_tensor_tensor(out=pre2[:], in0=modT[:, 32:40, :], scalar=1.0, in1=gain(64), op0=ALU.add, op1=ALU.mult))
                step(ve.tensor_tensor(post2[:], modT[:, 40:48, :], gain(72), ALU.mult))
                ve.tensor_tensor(post1[:], modT[:, 16:24, :], gain(56), ALU.mult).then_inc(mod_ready, 1)
                dve.wait_ge(lam_exp, l + 1)
                step(ve.tensor_tensor(lame[:, 2:3], lame[:, 1:2], lame[:, 0:1], ALU.subtract))
                step(ve.tensor_tensor(lame[:, 3:4], lame[:, 2:3], lamc[:, 0:1], ALU.subtract))

                def rotate(dst, swapped, cos, sin, tmp):
                    step(ve.tensor_tensor(tmp, swapped, sin, ALU.mult))
                    step(ve.tensor_tensor(dst, dst, cos, ALU.mult))
                    return ve.tensor_tensor(dst, dst, tmp, ALU.add)

                rope4 = rope_t.rearrange("p (h s) -> p h s", h=4)
                for i, dst in ((2, qA), (3, qB), (4, kB)):
                    b = prep(i).rearrange("p (h s) -> p h s", h=4)
                    rotate(dst[:, :, P:T], b, per_column(cst["cos_ab"], [P, 4, P], 1), per_column(cst["sin_ab"], [P, 4, P], 1), rope4).then_inc(prep_ev, 1)
                    dve.wait_ge(prep_ev, l * PREP_JOBS + i + 1)
                b = prep(5)
                step(rotate(kA[:, P:T], b[:, 0:P], cst["cos_ab"], cst["sin_ab"], rope_t[:, 0:P]))
                rk = slice(C_NOPE, C_QK)
                step(rotate(kC[rk, 0, P:T], b[rk, P:T], cst["cos_c"][rk, :], cst["sin_c"][rk, :], rope_t[rk, P:T]))
                ve.tensor_copy(kC[rk, 1:C_HEADS, 0:T], kC[rk, 0:1, 0:T].broadcast_to([C_ROPE, C_HEADS - 1, T])).then_inc(prep_ev, 1)
                b = prep(6)
                ve.tensor_copy(state[:, 0:512], b).then_inc(prep_ev, 1)
                r = rstd(1, PS[:, 7, 0:T], Q_LORA, norm_scratch(19968, T))
                step(ve.scalar_tensor_tensor(out=qcn[:, 0, :], in0=qcT[:, 0, :], scalar=parT[:, 80:81], in1=r, op0=ALU.mult, op1=ALU.mult))
                ve.scalar_tensor_tensor(out=qcn[:, 1, :], in0=qcT[:, 1, :], scalar=parT[:, 81:82], in1=r, op0=ALU.mult, op1=ALU.mult).then_inc(lora_ready, 1)
                dve.wait_ge(lora_ready, l * 2 + 1)
                r = rstd(2, PS[:, 7, 0:T], KV_LORA, norm_scratch(19968, T))
                ve.scalar_tensor_tensor(out=ckvT[:, 0:T], in0=kvcT, scalar=parT[:, 82:83], in1=r, op0=ALU.mult, op1=ALU.mult).then_inc(lora_ready, 1)
                for i in range(4):
                    b = prep(7 + i)
                    ve.tensor_copy(qC[0:C_QK, 2 * i:2 * i + 2, :], b[0:C_QK, :].rearrange("p (h t) -> p h t", h=2)).then_inc(prep_ev, 1)
                dve.wait_ge(prep_ev, l * PREP_JOBS + 11)
                qk = slice(0, C_QK)
                for i in range(2):
                    b = prep(11 + i)[qk].rearrange("p (h s) -> p h s", h=4)
                    rotate(qC[qk, 4 * i:4 * i + 4, P:T], b, per_column(cst["cos_c"][qk, :], [C_QK, 4, P], 1),
                           per_column(cst["sin_c"][qk, :], [C_QK, 4, P], 1), rope4[qk]).then_inc(prep_ev, 1)
                    dve.wait_ge(prep_ev, l * PREP_JOBS + 12 + i)
                b = prep(13)
                step(ve.tensor_copy(state[:, 512:768], b[:, 0:2 * P]))
                ve.tensor_copy(state[:, 768:800], b[:, 2 * P + C_NOPE:2 * P + C_QK]).then_inc(prep_ev, 1)
                for h in range(C_HEADS):
                    b = prep(14 + h)
                    ve.tensor_copy(kC[0:C_NOPE, h, :], b[0:C_NOPE, 0:384]).then_inc(prep_ev, 1)
                for t in range(3):
                    b = prep(22 + t)
                    ve.tensor_copy(vC[:, t, :], b).then_inc(prep_ev, 1)

                def finish_gate(g):
                    dve.wait_ge(z_ev, l * projections_out(Z_JOBS - 1) + projections_out(Z_GL + g))
                    v = gates[:, 2 * g:2 * g + 2, :]
                    step(ve.tensor_scalar(v, v, 1.0, None, ALU.add))
                    ve.reciprocal(v, v).then_inc(gate_ready, 1)

                def row_maxima(u):
                    br, t, g = ATT[u]
                    dve.wait_ge(scores_done, l * UNITS + u + 1)
                    b = 2 + 2 * (u % 2)
                    n, kn = (4, P) if t == 0 else (2, 2 * P)
                    scale = (C_QK if br == "C" else HD) ** -0.5
                    m = negm[:, u % 2, 0:n]
                    if br == "B":
                        s = PS[:, b:b + 2, 0:(n // 2) * kn].rearrange("p m (j k) -> p m j k", k=kn)
                        step(ve.reduce_max(m.rearrange("p (m j) -> p m j", m=2), s, X))
                    else:
                        step(ve.reduce_max(m, PS[:, b, :].rearrange("p (i k) -> p i k", k=kn), X))
                    if br == "A":
                        ns = nsink[:, n * g:n * g + n]
                        step(ve.scalar_tensor_tensor(out=m, in0=m, scalar=-scale, in1=ns, op0=ALU.mult, op1=ALU.min))
                        ve.tensor_tensor(sinke[:, u % 2, 0:n], m, ns, ALU.subtract).then_inc(negm_ready, 1)
                    else:
                        ve.tensor_scalar(m, m, -scale, None, ALU.mult).then_inc(negm_ready, 1)

                def normalise(u):
                    br, t, g = ATT[u]
                    n, kn = (4, P) if t == 0 else (2, 2 * P)
                    dve.wait_ge(prob_exp, (l * UNITS + u + 1) * 4)
                    s, r = psums[:, u % 2, 0:n], prec[:, u % 2, 0:n]
                    if br == "A":
                        dve.wait_ge(sink_exp, l * 6 + u + 1)
                        step(ve.tensor_tensor(s, s, sinke[:, u % 2, 0:n], ALU.add))
                    step(ve.reciprocal(r, s))
                    if br == "B":
                        step(ve.tensor_scalar(r[:, n // 2:n], r[:, n // 2:n], lame[:, 3:4], None, ALU.mult))
                    pr = prob[:, u % 2, :].rearrange("p (i k) -> p i k", k=kn)
                    ins = ve.tensor_tensor(pr, pr, per_column(r, [P, n, kn], 2), ALU.mult)
                    if br == "B":
                        step(ins)
                        ins = ve.tensor_tensor(prob[:, u % 2, 0:T], prob[:, u % 2, 0:T], prob[:, u % 2, T:2 * T], ALU.add)
                    ins.then_inc(prob_ready, 1)

                def heads_out(u):
                    br, t, g = ATT[u]
                    dve.wait_ge(pv_done, l * UNITS + u + 1)
                    q_ = {"A": qA, "B": qB, "C": qC}[br]
                    if t == 0:
                        ins = ve.tensor_copy(q_[:, 2 * g:2 * g + 2, 0:P], PS[:, 7, 0:T].rearrange("p (h s) -> p h s", h=2))
                    else:
                        ins = ve.tensor_copy(q_[:, g, P:T], PS[:, 7, 0:P])
                    ins.then_inc(o_ready, 1)

                for s in range(UNITS + 3):
                    if s < UNITS:
                        row_maxima(s)
                    if s >= 3:
                        heads_out(s - 3)
                    if 1 <= s <= UNITS:
                        normalise(s - 1)
                    if s % 2 == 1 and s // 2 + 4 < 12:
                        finish_gate(s // 2 + 4)
                    if s % 4 == 0 and 4 <= s <= 16:
                        finish_gate(s // 4 - 1)

                r = rstd(3, PS[:, 4:6, :].rearrange("p a b -> p (a b)"), P, norm_scratch(12288, 4 * T))
                ve.scalar_tensor_tensor(out=qB, in0=qB, scalar=subl[:, 0:1], in1=r.rearrange("p (h t) -> p h t", h=4),
                                        op0=ALU.mult, op1=ALU.mult).then_inc(od_ready, 1)
                dve.wait_ge(od_ready, l + 1)
                for j in range(KC):
                    dve.wait_ge(branch_done, l * KC + j + 1)
                    b = 2 * (j % 2)
                    m = merged[:, j, :]
                    step(ve.tensor_tensor(m, PS[:, b, 0:T], gates[:, j, :], ALU.mult))
                    step(ve.tensor_tensor(merge_t[:, 0, :], PS[:, b, T:2 * T], gates[:, 16 + j, :], ALU.mult))
                    step(ve.tensor_tensor(merge_t[:, 1, :], PS[:, b + 1, 0:T], gates[:, 8 + j, :], ALU.mult))
                    step(ve.tensor_tensor(m, m, merge_t[:, 0, :], ALU.add))
                    ve.tensor_tensor(m, m, merge_t[:, 1, :], ALU.add).then_inc(merged_ready, 1)
                    dve.wait_ge(merged_ready, l * KC + j + 1)
                add_normalised(4, aT, PS[:, 0, 0:T], post1, norm_scratch(8192, T), x1_ready)
                dve.wait_ge(x1_ready, (l + 1) * 2 * KC)
                normalise_x(5, h2T, PS[:, 1, 0:T], norm_scratch(8192, T))

                both = [P, 2, N_EXPERTS]
                FAR = 3.0e38
                for v in (r_gs[:, :, 8:12], r_mask[:, :, N_EXPERTS:N_EXPERTS + 2]):
                    step(ve.memset(v, -FAR))
                dve.wait_ge(route_exp, l + 1)
                step(ve.tensor_scalar(r_score, r_score, 1.0, None, ALU.add))
                step(ve.reciprocal(r_score, r_score))
                step(ve.tensor_tensor(r_bias, r_score, per_column(rbias[:], both, 1), ALU.add), own=True)
                for t in range(2):
                    for g in range(N_GROUPS):
                        step.add(ve.max(r_top[:, t * N_GROUPS + g, :], r_bias[:, t, 8 * g:8 * g + 8]))
                dve.wait_ge(vector_step, step.base + step.n)
                tops = r_top.rearrange("p (t g) k -> p t g k", t=2)
                step(ve.tensor_tensor(r_gs[:, :, 0:8], tops[:, :, :, 0], tops[:, :, :, 1], ALU.add), own=True)
                for t in range(2):
                    step.add(ve.max(r_g8[:, t, :], r_gs[:, t, 0:8]))
                dve.wait_ge(vector_step, step.base + step.n)
                step(ve.memset(r_g8[:, :, TOPK_GROUPS:8], -FAR), own=True)
                for t in range(2):
                    step.add(ve.match_replace(out=r_grep[:, t, :], in_to_replace=r_g8[:, t, :], in_values=r_gs[:, t, :], imm_value=FAR))
                dve.wait_ge(vector_step, step.base + step.n)
                step(ve.tensor_scalar(r_gm, r_grep[:, :, 0:8], FAR / 2, None, ALU.is_ge))
                grouped = [P, 2, N_GROUPS, 8]
                for t in range(2):
                    step(ve.tensor_tensor(r_mask[:, t, 0:N_EXPERTS].rearrange("p (g k) -> p g k", g=8), r_bias[:, t, :].rearrange("p (g k) -> p g k", g=8),
                                          per_column(r_gm[:, t, :], grouped[0:1] + grouped[2:], 2), ALU.mult))
                step(ve.tensor_scalar(r_gm, r_gm, 1e30, -1e30, ALU.mult, ALU.add))
                for t in range(2):
                    v = r_mask[:, t, 0:N_EXPERTS].rearrange("p (g k) -> p g k", g=8)
                    step(ve.tensor_tensor(v, v, per_column(r_gm[:, t, :], grouped[0:1] + grouped[2:], 2), ALU.add), own=True)
                for t in range(2):
                    step.add(ve.max(r_m8[:, t, :], r_mask[:, t, 0:N_EXPERTS]))
                dve.wait_ge(vector_step, step.base + step.n)
                step(ve.memset(r_m8[:, :, TOP_K:8], -FAR), own=True)
                for t in range(2):
                    step.add(ve.match_replace(out=r_mrep[:, t, :], in_to_replace=r_m8[:, t, :], in_values=r_mask[:, t, :], imm_value=FAR))
                dve.wait_ge(vector_step, step.base + step.n)
                ve.tensor_scalar(sel[:], r_mrep[:, :, 0:N_EXPERTS], FAR / 2, None, ALU.is_ge).then_inc(sel_ready, 1)
                dve.wait_ge(sel_ready, l + 1)
                dve.wait_ge(rank_done, l + 1)
                step(ve.tensor_copy(rank[:], PS[:, 1, 0:128].rearrange("p (t e) -> p t e", t=2)))
                step(ve.tensor_copy(count[:], PS[:, 1, 128:192]))
                step(ve.reduce_max(r_most, count[:], X))
                step(ve.tensor_scalar(r_np, r_most, CAP + 0.5, 1.0, ALU.is_gt, ALU.add))
                for k in (2, 3):
                    step(ve.scalar_tensor_tensor(out=r_np, in0=r_most, scalar=k * CAP + 0.5, in1=r_np, op0=ALU.is_gt, op1=ALU.add))
                ve.tensor_copy(npass_i[:], r_np).then_inc(npass_ready, 1)
                step(ve.tensor_tensor(gatew[:], r_score, sel[:], ALU.mult))
                step(ve.reduce_sum(r_sum, gatew[:], X))
                step(ve.reciprocal(r_sum, r_sum))
                step(ve.tensor_scalar(r_sum, r_sum, ROUTED_SCALE, None, ALU.mult))
                step(ve.tensor_tensor(gatew[:], gatew[:], per_column(r_sum, both, 2), ALU.mult))

                dve.wait_ge(shared_exp, l + 1)
                dve.wait_ge(shared_gu, l + 1)
                step(ve.tensor_scalar(ssig, ssig, 1.0, None, ALU.add))
                step(ve.reciprocal(ssig, ssig))
                step(ve.tensor_tensor(ssig, PS[:, 6, :].rearrange("p (f t) -> p f t", f=2), ssig, ALU.mult))
                ve.tensor_tensor(view(0, 2, T), PS[:, 7, :].rearrange("p (f t) -> p f t", f=2), ssig, ALU.mult).then_inc(shared_hid, 1)

                ve.memset(xs[:, :, CAP + SLOTS:XSW], 0.0).then_inc(pad_set, 1)
                dve.wait_ge(state_out, (l + 1) * 6 * 16)
                step(ve.memset(r_scan[:, :, 0:33], 0.0))
                dve.wait_ge(npass_ready, l + 1)
                apart(dve)
                npass = dve.value_load(npass_i[0:1, 0:1], min_val=1, max_val=4)
                dve.sem_inc(params_free, 1)
                assert step.n == VECTOR_STEPS, step.n

                with dve.Fori(0, npass) as p:
                    q = dve.snap(before_l + p)
                    pstep = Chain(pass_step, q * PASS_STEPS)
                    pstep(ve.scalar_tensor_tensor(out=r_selp, in0=rank[:], scalar=0.0, in1=sel[:], op0=ALU.is_ge, op1=ALU.mult))
                    pstep(ve.scalar_tensor_tensor(out=r_selp, in0=rank[:], scalar=CAP - 0.5, in1=r_selp, op0=ALU.is_lt, op1=ALU.mult))
                    pstep(ve.tensor_scalar(r_cnt, count[:], 0.0, float(CAP), ALU.max, ALU.min))
                    pstep(ve.tensor_copy(r_scan[:, 0, 33:96], r_cnt[:, 0:63]))
                    for k in range(6):
                        s, d = k % 2, 1 - k % 2
                        pstep(ve.tensor_tensor(r_scan[:, d, 32:96], r_scan[:, s, 32:96], r_scan[:, s, 32 - 2 ** k:96 - 2 ** k], ALU.add))
                    off = r_scan[:, 0, 32:96]
                    ve.tensor_copy(off_i[:], off).then_inc(off_ready, 1)
                    pstep(ve.tensor_tensor(r_val, rank[:], per_column(off, both, 1), ALU.add))
                    pstep(ve.scalar_tensor_tensor(out=r_val, in0=r_val, scalar=1.0, in1=r_selp, op0=ALU.add, op1=ALU.mult))
                    pstep(ve.tensor_scalar(r_val, r_val, -1.0, None, ALU.add))
                    pstep(ve.tensor_tensor(r_gwp, gatew[:], r_selp, ALU.mult), own=True)
                    for t in range(2):
                        pstep.add(ve.max(r_pos[:, t, :], r_val[:, t, :]))
                    dve.wait_ge(pass_step, pstep.base + pstep.n)
                    for t in range(2):
                        for k in range(TOP_K):
                            pstep(ve.scalar_tensor_tensor(out=r_junk, in0=r_val[:, t, :], scalar=r_pos[:, t, k:k + 1], in1=r_gwp[:, t, :],
                                                          op0=ALU.is_equal, op1=ALU.mult, accum_out=r_wk[:, t, k:k + 1]))
                    for blk in range(NSB):
                        if blk:
                            pstep(ve.tensor_scalar(r_pos, r_pos, -float(SB), None, ALU.add))
                            dve.wait_ge(gvt_tr, q * 2 * NSB + 2 * blk)
                        for t in range(2):
                            pstep(ve.tensor_scalar(gval[:, t, :], iota, r_pos[:, t, 0:1], r_wk[:, t, 0:1], ALU.is_equal, ALU.mult))
                            for k in range(1, TOP_K):
                                pstep(ve.tensor_scalar(r_tmp, iota, r_pos[:, t, k:k + 1], r_wk[:, t, k:k + 1], ALU.is_equal, ALU.mult))
                                pstep(ve.tensor_tensor(gval[:, t, :], gval[:, t, :], r_tmp, ALU.add))
                        if blk:
                            dve.wait_ge(gather_done, q * NSB * KC + KC * blk)
                        ve.tensor_scalar(gsel, gval, 0.0, None, ALU.is_gt).then_inc(g_ready, 1)
                    pstep(ve.tensor_scalar(rank[:], rank[:], -float(CAP), None, ALU.add))
                    pstep(ve.tensor_scalar(count[:], count[:], -float(CAP), None, ALU.add))
                    assert pstep.n == PASS_STEPS, pstep.n

                    def hidden(e, odd):
                        chain = Chain(expert_step, (q * N_EXPERTS + e) * 3)
                        dve.wait_ge(sig_ready, q * N_EXPERTS + e + 1)
                        s = sig[:, odd, :]
                        chain(ve.tensor_scalar(s, s, 1.0, None, ALU.add))
                        chain(ve.reciprocal(s, s))
                        chain(ve.tensor_tensor(act_g, PS[:, odd, 0:P], s, ALU.mult))
                        ve.tensor_tensor(hid_rows[:, odd, :], PS[:, odd, P:2 * P], act_g, ALU.mult).then_inc(hid_ready, 1)

                    def copy_hidden(e, odd, waits=True):
                        dve.wait_ge(hid_tr, q * N_EXPERTS + e + 1)
                        if waits:
                            dve.wait_ge(down_done, q * N_EXPERTS + e - 1)
                        ve.tensor_copy(hid[:, odd, :], PS[:, 6 + odd, 0:P]).then_inc(hidT_ready, 1)

                    hidden(0, 0)
                    for e in range(2):
                        copy_hidden(e, e, waits=False)
                        hidden(e + 1, 1 - e)
                    with dve.Fori(0, N_EXPERTS // 2 - 2) as i:
                        for u in range(2):
                            copy_hidden(i * 2 + (2 + u), u)
                            hidden(i * 2 + (3 + u), 1 - u)
                    e = N_EXPERTS - 2
                    copy_hidden(e, 0)
                    hidden(e + 1, 1)
                    copy_hidden(e + 1, 1)
                    dve.wait_ge(y_shared, l * 4 + 4)
                    dve.wait_ge(comb_done, (q + 1) * 12)
                    for j in range(4):
                        v = yT[:, 2 * j:2 * j + 2, :]
                        ve.tensor_tensor(v, v, PS[:, j, :].rearrange("p (c t) -> p c t", c=2), ALU.add).then_inc(y_ready, 1)
                    dve.wait_ge(y_ready, (q + 1) * 4)
                dve.reg_add(passes, passes, npass)
                step = Chain(tail_step, l * TAIL_STEPS)
                add_normalised(6, yT, PS[:, 4, 0:T], post2, norm_scratch(15360, T), x_ready)
                assert step.n == TAIL_STEPS, step.n


_INS = ["x_prompt", "x_sample", "cache_swa_k", "cache_swa_v", "cache_dif_k", "cache_dif_v", "cache_mla_ckv",
        "cache_mla_kpe", "c", "c_ctx", "w_mod", "b_mod", "norm_attn_pre", "norm_attn_post", "norm_ffn_pre",
        "norm_ffn_post", "w_in", "swa_sink", "dif_lq1", "dif_lk1", "dif_lq2", "dif_lk2", "dif_subln", "mla_q_norm",
        "mla_w_uq", "mla_kv_norm", "mla_w_ukv", "w_branch_a", "w_branch_b", "w_branch_c", "w_out", "router_w",
        "router_bias", "moe_w_gate", "moe_w_up", "moe_w_down", "shared_w_gate", "shared_w_up", "shared_w_down"]
_OUTS = {"y_prompt": (1, P, D), "y_sample": (1, P, D), "swa_k": (1, DEPTH, P, A_KV, HD), "swa_v": (1, DEPTH, P, A_KV, HD),
         "dif_k": (1, DEPTH, P, B_HEADS, 2, HD), "dif_v": (1, DEPTH, P, B_HEADS, 2 * HD), "ckv": (1, DEPTH, P, KV_LORA),
         "kpe": (1, DEPTH, P, C_ROPE)}


def kernel(**inputs):
    import concourse.bacc as bacc
    from concourse.bass_utils import run_bass_kernel_spmd

    nc = bacc.Bacc("TRN2", target_bir_lowering=False, num_devices=1)
    tables, lams = constants()
    arrays = {name: np.ascontiguousarray(inputs[name]) for name in _INS}
    arrays["consts"], arrays["lam_consts"] = tables, lams
    ins = {name: nc.dram_tensor(f"in_{name}", v.shape, mybir.dt.from_np(v.dtype), kind="ExternalInput").ap()
           for name, v in arrays.items()}
    outs = {name: nc.dram_tensor(f"out_{name}", shape, F32, kind="ExternalOutput").ap() for name, shape in _OUTS.items()}
    hybrid_layers(nc, ins, outs)
    r = run_bass_kernel_spmd(nc, [{f"in_{name}": v for name, v in arrays.items()}], core_ids=[0])
    return tuple(r.results[0][f"out_{name}"] for name in _OUTS)
```
